# Optimizing a Trainium2 kernel written in Bass

```python
import math
import jax, jax.numpy as jnp
from jax import lax
import numpy as np

D_MODEL = 1024
BATCH = 1
SEQ = 2048
DEPTH = 2

N_A_LAYERS = DEPTH // 2
N_B_LAYERS = DEPTH - N_A_LAYERS

A_HEADS = 8
A_DK = 128
A_DV = 128
A_QK = A_HEADS * A_DK
A_V = A_HEADS * A_DV
A_CONV = 4
A_CONV_CH = 2 * A_QK + A_V
A_CHUNK = 64
A_IN = 2 * A_QK + 2 * A_V + 2 * A_HEADS

B_HEADS = 16
B_DH = 64
B_W = B_HEADS * B_DH
B_BLOCK = 128
B_IN = 2 * B_W
KV_IN = 2 * B_W + B_HEADS

NORM_EPS = 1e-6

kernel_name = "yoco_gdn_fox_sandwich_adaln"

def rms_norm(x, gain):
    xf = x.astype(jnp.float32)
    y = xf * lax.rsqrt(jnp.mean(xf * xf, axis=-1, keepdims=True) + NORM_EPS)
    return (y * gain.astype(jnp.float32)).astype(x.dtype)

def l2_norm(x):
    xf = x.astype(jnp.float32)
    return xf * lax.rsqrt(jnp.sum(xf * xf, axis=-1, keepdims=True) + NORM_EPS)

def adaln(c, w, b, n):
    m = jax.nn.silu(c) @ w + b
    return [t[:, None, :] for t in jnp.split(m, n, axis=-1)]

def causal_dwconv_silu(x, w):
    k_w, ch = w.shape
    y = lax.conv_general_dilated(
        x, w[:, None, :].astype(x.dtype), window_strides=(1,), padding=[(k_w - 1, 0)],
        dimension_numbers=('NWC', 'WIO', 'NWC'), feature_group_count=ch)
    return jax.nn.silu(y)

def gated_delta_rule(q, k, v, g, beta):
    bsz, seq, heads, dk = q.shape
    dv = v.shape[-1]
    n_chunks = seq // A_CHUNK
    f32 = jnp.float32

    def to_chunks(t):
        t = t.astype(f32).reshape((bsz, n_chunks, A_CHUNK, heads) + t.shape[3:])
        return jnp.moveaxis(t, (1, 3), (0, 2))

    q_c = to_chunks(q) * (dk ** -0.5)
    k_c = to_chunks(k)
    v_c = to_chunks(v)
    b_c = to_chunks(beta)
    g_c = jnp.cumsum(to_chunks(g), axis=-1)
    tri = jnp.tril(jnp.ones((A_CHUNK, A_CHUNK), dtype=bool))
    decay = jnp.exp(jnp.where(tri, g_c[..., :, None] - g_c[..., None, :], -jnp.inf))

    k_beta = k_c * b_c[..., None]
    a_strict = jnp.tril(jnp.einsum('nbhid,nbhjd->nbhij', k_beta, k_c) * decay, -1)
    rhs = jnp.concatenate([v_c * b_c[..., None], k_beta * jnp.exp(g_c)[..., None]], axis=-1)
    sol = lax.linalg.triangular_solve(a_strict + jnp.eye(A_CHUNK, dtype=f32), rhs,
                                      left_side=True, lower=True, unit_diagonal=True)
    u_c, w_c = sol[..., :dv], sol[..., dv:]
    qk = jnp.einsum('nbhid,nbhjd->nbhij', q_c, k_c) * decay

    def step(state, inp):
        q_i, k_i, u_i, w_i, g_i, qk_i = inp
        v_new = u_i - jnp.einsum('bhck,bhkv->bhcv', w_i, state)
        o_i = (jnp.einsum('bhck,bhkv->bhcv', q_i * jnp.exp(g_i)[..., None], state)
               + jnp.einsum('bhij,bhjv->bhiv', qk_i, v_new))
        g_last = g_i[..., -1:]
        state = (state * jnp.exp(g_last)[..., None]
                 + jnp.einsum('bhck,bhcv->bhkv', k_i * jnp.exp(g_last - g_i)[..., None], v_new))
        return state, o_i

    s0 = jnp.zeros((bsz, heads, dk, dv), f32)
    _, o = lax.scan(step, s0, (q_c, k_c, u_c, w_c, g_c, qk))
    return jnp.moveaxis(o, (0, 2), (1, 3)).reshape(bsz, seq, heads, dv)

def gated_deltanet(h, w_in, conv_w, a_log, dt_bias, o_gain, w_out):
    bsz, seq, _ = h.shape
    proj = h @ w_in
    qkv, z, a, b = jnp.split(proj, [A_CONV_CH, A_CONV_CH + A_V, A_CONV_CH + A_V + A_HEADS], axis=-1)
    qkv = causal_dwconv_silu(qkv, conv_w)
    q, k, v = jnp.split(qkv, [A_QK, 2 * A_QK], axis=-1)
    q = l2_norm(q.reshape(bsz, seq, A_HEADS, A_DK))
    k = l2_norm(k.reshape(bsz, seq, A_HEADS, A_DK))
    v = v.reshape(bsz, seq, A_HEADS, A_DV)
    beta = jax.nn.sigmoid(b.astype(jnp.float32))
    g = -jnp.exp(a_log.astype(jnp.float32)) * jax.nn.softplus(a.astype(jnp.float32) + dt_bias.astype(jnp.float32))
    o = gated_delta_rule(q, k, v, g, beta)
    o = rms_norm(o, o_gain).astype(h.dtype).reshape(bsz, seq, A_V)
    return (o * jax.nn.silu(z)) @ w_out

def shared_kv(x, c, mod_w, mod_b, norm_g, w_kvf, b_f):
    bsz, seq, _ = x.shape
    shift, scale = adaln(c, mod_w, mod_b, 2)
    h = rms_norm(x, norm_g) * (1 + scale) + shift
    k, v, f = jnp.split(h @ w_kvf, [B_W, 2 * B_W], axis=-1)
    k = k.reshape(bsz, seq, B_HEADS, B_DH).transpose(0, 2, 1, 3)
    v = v.reshape(bsz, seq, B_HEADS, B_DH).transpose(0, 2, 1, 3)
    log_f = jax.nn.log_sigmoid(f.astype(jnp.float32) + b_f.astype(jnp.float32))
    log_f_cum = jnp.cumsum(log_f, axis=1).transpose(0, 2, 1)
    return k, v, log_f_cum

def forgetting_attention(h, w_in, w_out, k, v, log_f_cum):
    bsz, seq, _ = h.shape
    q, z = jnp.split(h @ w_in, 2, axis=-1)
    q = q.reshape(bsz, seq, B_HEADS, B_DH).transpose(0, 2, 1, 3) * (B_DH ** -0.5)
    outs = []
    for blk in range(seq // B_BLOCK):
        s0 = blk * B_BLOCK
        s1 = s0 + B_BLOCK
        logits = (jnp.einsum('bhqd,bhkd->bhqk', q[:, :, s0:s1], k[:, :, :s1]).astype(jnp.float32)
                  + log_f_cum[:, :, s0:s1, None] - log_f_cum[:, :, None, :s1])
        causal = jnp.arange(s0, s1)[:, None] >= jnp.arange(s1)[None, :]
        p = jax.nn.softmax(jnp.where(causal, logits, -jnp.inf), axis=-1)
        outs.append(jnp.einsum('bhqk,bhkd->bhqd', p.astype(v.dtype), v[:, :, :s1]))
    o = jnp.concatenate(outs, axis=2).transpose(0, 2, 1, 3).reshape(bsz, seq, B_W)
    return (o * jax.nn.silu(z)) @ w_out

def setup_inputs(seed: int = 0) -> dict:
    key = jax.random.key(seed)
    ks = iter(jax.random.split(key, 40))
    D = D_MODEL
    na, nb = N_A_LAYERS, N_B_LAYERS

    def nrm(shape, scale):
        return scale * jax.random.normal(next(ks), shape, jnp.float32)

    x = nrm((BATCH, SEQ, D), 1.0)
    c = nrm((BATCH, D), 1.0)
    a_mod_w = nrm((na, D, 3 * D), 0.5 * D ** -0.5)
    a_mod_b = nrm((na, 3 * D), 0.02)
    a_pre_g = 1.0 + nrm((na, D), 0.05)
    a_post_g = 1.0 + nrm((na, D), 0.05)
    a_w_in = nrm((na, D, A_IN), D ** -0.5)
    a_conv_w = nrm((na, A_CONV, A_CONV_CH), A_CONV ** -0.5)
    a_a_log = jnp.log(jax.random.uniform(next(ks), (na, A_HEADS), jnp.float32, 1.0, 16.0))
    dt = jnp.exp(jax.random.uniform(next(ks), (na, A_HEADS), jnp.float32, math.log(1e-3), math.log(0.1)))
    a_dt_bias = dt + jnp.log(-jnp.expm1(-dt))
    a_o_gain = 1.0 + nrm((na, A_DV), 0.05)
    a_w_out = nrm((na, A_V, D), A_V ** -0.5)
    kv_mod_w = nrm((D, 2 * D), 0.5 * D ** -0.5)
    kv_mod_b = nrm((2 * D,), 0.02)
    kv_norm_g = 1.0 + nrm((D,), 0.05)
    kv_w = jnp.concatenate([nrm((D, 2 * B_W), D ** -0.5), nrm((D, B_HEADS), 0.1 * D ** -0.5)], axis=1)
    kv_b_f = jax.random.uniform(next(ks), (B_HEADS,), jnp.float32, 1.0, 6.0)
    b_mod_w = nrm((nb, D, 3 * D), 0.5 * D ** -0.5)
    b_mod_b = nrm((nb, 3 * D), 0.02)
    b_pre_g = 1.0 + nrm((nb, D), 0.05)
    b_post_g = 1.0 + nrm((nb, D), 0.05)
    b_w_in = nrm((nb, D, B_IN), D ** -0.5)
    b_w_out = nrm((nb, B_W, D), B_W ** -0.5)
    return {"x": x, "c": c,
            "a_mod_w": a_mod_w, "a_mod_b": a_mod_b, "a_pre_g": a_pre_g, "a_post_g": a_post_g,
            "a_w_in": a_w_in, "a_conv_w": a_conv_w, "a_a_log": a_a_log, "a_dt_bias": a_dt_bias,
            "a_o_gain": a_o_gain, "a_w_out": a_w_out,
            "kv_mod_w": kv_mod_w, "kv_mod_b": kv_mod_b, "kv_norm_g": kv_norm_g, "kv_w": kv_w,
            "kv_b_f": kv_b_f,
            "b_mod_w": b_mod_w, "b_mod_b": b_mod_b, "b_pre_g": b_pre_g, "b_post_g": b_post_g,
            "b_w_in": b_w_in, "b_w_out": b_w_out}

def reference(x, c, a_mod_w, a_mod_b, a_pre_g, a_post_g, a_w_in, a_conv_w, a_a_log, a_dt_bias,
              a_o_gain, a_w_out, kv_mod_w, kv_mod_b, kv_norm_g, kv_w, kv_b_f,
              b_mod_w, b_mod_b, b_pre_g, b_post_g, b_w_in, b_w_out):
    k_sh = v_sh = f_cum = None
    for layer in range(DEPTH):
        if layer < N_A_LAYERS:
            j = layer
            shift, scale, gate = adaln(c, a_mod_w[j], a_mod_b[j], 3)
            h = rms_norm(x, a_pre_g[j]) * (1 + scale) + shift
            y = gated_deltanet(h, a_w_in[j], a_conv_w[j], a_a_log[j], a_dt_bias[j], a_o_gain[j], a_w_out[j])
            x = x + gate * rms_norm(y, a_post_g[j])
            if layer == N_A_LAYERS - 1:
                k_sh, v_sh, f_cum = shared_kv(x, c, kv_mod_w, kv_mod_b, kv_norm_g, kv_w, kv_b_f)
        else:
            j = layer - N_A_LAYERS
            shift, scale, gate = adaln(c, b_mod_w[j], b_mod_b[j], 3)
            h = rms_norm(x, b_pre_g[j]) * (1 + scale) + shift
            y = forgetting_attention(h, b_w_in[j], b_w_out[j], k_sh, v_sh, f_cum)
            x = x + gate * rms_norm(y, b_post_g[j])
    return x


_drawn_inputs = setup_inputs


def setup_inputs(seed=0):
    import zlib

    import numpy as np

    out = dict(_drawn_inputs(seed))
    spreads = {}
    factors = {'a_post_g': 3.306,
     'a_o_gain': 3.317,
     'kv_mod_b': 3.79,
     'kv_norm_g': 4.288,
     'b_mod_b': 2.873,
     'b_pre_g': 3.5,
     'b_post_g': 3.694}
    for name, (base, spread) in spreads.items():
        noise = np.random.default_rng([zlib.crc32(name.encode()), seed]).standard_normal(out[name].shape)
        drawn = base * np.exp(spread * noise) if base else spread * noise
        out[name] = __import__('jax').numpy.asarray(drawn.astype(out[name].dtype))
    for name, factor in factors.items():
        out[name] = (out[name] * factor).astype(out[name].dtype)
    return out
```

```python
from contextlib import ExitStack
from math import log

import concourse.bass as bass
from concourse import mybir

F32 = mybir.dt.float32
F32R = mybir.dt.float32r
BF16 = mybir.dt.bfloat16
U8 = mybir.dt.uint8
ALU = mybir.AluOpType
ACT = mybir.ActivationFunctionType
AX = mybir.AxisListType

P = 128
D = 1024
KC = D // P
SEQ = 2048
BLK = 512
NB = SEQ // BLK
NT = SEQ // P
AH = 8
BH = 16
DH = 64
EPS = 1e-6
BIG = 1.0e30


class Stage:

    def __init__(self, nc, name):
        self.nc, self.name, self.ctx, self.sems = nc, name, ExitStack(), []

    def __enter__(self):
        self.ctx.__enter__()
        return self

    def __exit__(self, *e):
        self.ctx.__exit__(*e)
        self.nc.clear_and_free_semaphores(self.sems)
        self.nc.all_engine_barrier()

    def sb(self, name, shape, dt=F32):
        return self.ctx.enter_context(self.nc.sbuf_tensor(f"{self.name}_{name}", shape, dt))

    def ps(self, name, shape, dt=F32):
        return self.ctx.enter_context(self.nc.psum_tensor(f"{self.name}_{name}", shape, dt))

    def sem(self, name):
        self.sems.append(self.nc.alloc_semaphore(f"{self.name}_{name}"))
        return self.sems[-1]

    def pool_sem(self, name):
        return self.nc.alloc_semaphore(f"{self.name}_{name}")

    def block(self):
        return self.ctx.enter_context(self.nc.Block())


class Steps:

    def __init__(self, eng, sem):
        self.eng, self.sem, self.base, self.n = eng, sem, 0, 0

    def restart(self, base):
        self.base, self.n = base, 0

    def did(self, ins):
        ins.then_inc(self.sem, 1)
        self.n += 1

    def wait(self):
        self.eng.wait_ge(self.sem, self.base + self.n)


def make_identity(pool, ident, sem):
    pool.memset(ident, 0.0).then_inc(sem, 1)
    pool.wait_ge(sem, 1)
    pool.affine_select(out=ident, in_=ident, compare_op=ALU.not_equal, fill=1.0, base=0,
                       pattern=[[-1, P]], channel_multiplier=1).then_inc(sem, 1)


def modulation(nc, c, weights, s_mod):
    pieces = [(w, b, j) for w, b in weights for j in range(w.shape[1] // D)]
    with Stage(nc, "mod") as st:
        ccol = st.sb("ccol", [P, KC])
        csil = st.sb("csil", [P, KC])
        w_sb = st.sb("w", [P, 3, KC, D])
        bias = st.sb("bias", [1, 2, D])
        row = st.sb("row", [1, 2, D])
        acc = st.ps("acc", [P, 2, 2, BLK])
        c_in, c_ready = st.sem("c_in"), st.sem("c_ready")
        w_in = [st.sem(f"w_in{s}") for s in range(3)]
        b_in = [st.pool_sem(f"b_in{s}") for s in range(2)]
        summed, added = st.sem("summed"), st.sem("added")
        stored = [st.pool_sem(f"stored{s}") for s in range(2)]
        block = st.block()

        @block.sync
        def _(sp):
            sp.dma_start(ccol[:, :], c).then_inc(c_in, 16)
            for n, (w, b, j) in enumerate(pieces):
                if n >= 3:
                    sp.wait_ge(summed, n - 2)
                sp.dma_start(w_sb[:, n % 3], w[:, j * D:(j + 1) * D].rearrange("(k p) f -> p k f", p=P))\
                  .then_inc(w_in[n % 3], 16)

        @block.gpsimd
        def _(pool):
            for n, (w, b, j) in enumerate(pieces):
                if n >= 2:
                    pool.wait_ge(added, n - 1)
                pool.dma_start(bias[:, n % 2], b[j * D:(j + 1) * D].rearrange("(o f) -> o f", o=1))\
                    .then_inc(b_in[n % 2], 16)
                if n >= 1:
                    pool.wait_ge(added, n)
                    pool.dma_start(s_mod[:, (n - 1) * D:n * D], row[:, (n - 1) % 2]).then_inc(stored[(n - 1) % 2], 16)
            n = len(pieces)
            pool.wait_ge(added, n)
            pool.dma_start(s_mod[:, (n - 1) * D:n * D], row[:, (n - 1) % 2]).then_inc(stored[(n - 1) % 2], 16)
            for s in range(2):
                pool.wait_ge(stored[s], 16 * (n // 2))

        @block.scalar
        def _(act):
            act.wait_ge(c_in, 16)
            nc.scalar.activation(csil[:, :], ccol[:, :], ACT.Silu).then_inc(c_ready, 1)

        @block.tensor
        def _(pe):
            pe.wait_ge(c_ready, 1)
            for n in range(len(pieces)):
                pe.wait_ge(w_in[n % 3], 16 * (n // 3 + 1))
                if n >= 2:
                    pe.wait_ge(added, n - 1)
                for half in range(2):
                    for k in range(KC):
                        ins = nc.tensor.matmul(acc[0:1, n % 2, half], csil[:, k:k + 1],
                                               w_sb[:, n % 3, k, half * BLK:(half + 1) * BLK],
                                               start=k == 0, stop=k == KC - 1)
                ins.then_inc(summed, 1)

        @block.vector
        def _(dve):
            for n in range(len(pieces)):
                dve.wait_ge(summed, n + 1)
                dve.wait_ge(b_in[n % 2], 16 * (n // 2 + 1))
                if n >= 2:
                    dve.wait_ge(stored[n % 2], 16 * (n // 2))
                nc.vector.tensor_tensor(row[:, n % 2], acc[0:1, n % 2].rearrange("p a b -> p (a b)"),
                                        bias[:, n % 2], ALU.add).then_inc(added, 1)


def normalize_input(nc, x, s_xnT):
    with Stage(nc, "nrm") as st:
        ident = st.sb("ident", [P, P])
        xt = st.sb("x", [P, 3, D])
        xn = st.sb("xn", [P, 2, D])
        junk = st.sb("junk", [P, D])
        ss = st.sb("ss", [P, NT])
        eps = st.sb("eps", [P, 1])
        rstd = st.sb("rstd", [P, NT])
        outT = st.sb("outT", [P, 2, D])
        turned = st.ps("turned", [P, 2, 2, BLK])
        x_in = [st.sem(f"x_in{s}") for s in range(3)]
        ident_ok, eps_ok, squared, logged, rooted = (st.sem(n) for n in ("ident_ok", "eps_ok", "squared", "logged", "rooted"))
        scaled, turned_ok, copied = (st.sem(n) for n in ("scaled", "turned_ok", "copied"))
        stored = [st.pool_sem(f"stored{s}") for s in range(2)]
        block = st.block()

        @block.sync
        def _(sp):
            for i in range(NT):
                if i >= 3:
                    sp.wait_ge(scaled, i - 2)
                sp.dma_start(xt[:, i % 3], x[0, i * P:(i + 1) * P, :]).then_inc(x_in[i % 3], 16)

        @block.gpsimd
        def _(pool):
            pool.memset(eps[:, :], EPS).then_inc(eps_ok, 1)
            make_identity(pool, ident[:, :], ident_ok)
            for i in range(NT):
                pool.wait_ge(copied, i + 1)
                pool.dma_start(s_xnT.rearrange("(k p) t -> p k t", p=P)[:, :, i * P:(i + 1) * P],
                               outT[:, i % 2].rearrange("p (k t) -> p k t", k=KC)).then_inc(stored[i % 2], 16)
            for s in range(2):
                pool.wait_ge(stored[s], 16 * (NT // 2))

        @block.scalar
        def _(act):
            act.wait_ge(eps_ok, 1)
            for i in range(NT):
                act.wait_ge(x_in[i % 3], 16 * (i // 3 + 1))
                if i:
                    act.wait_ge(squared, i)
                nc.scalar.activation(junk[:, :], xt[:, i % 3], ACT.Square, accum_out=ss[:, i:i + 1]).then_inc(squared, 1)
                act.wait_ge(squared, i + 1)
                nc.scalar.activation(ss[:, i:i + 1], ss[:, i:i + 1], ACT.Ln, bias=eps[:, :], scale=1.0 / D)\
                    .then_inc(logged, 1)
                act.wait_ge(logged, i + 1)
                nc.scalar.activation(rstd[:, i:i + 1], ss[:, i:i + 1], ACT.Exp, scale=-0.5).then_inc(rooted, 1)

        @block.vector
        def _(dve):
            for i in range(NT + 1):
                if i < NT:
                    dve.wait_ge(rooted, i + 1)
                    if i >= 2:
                        dve.wait_ge(turned_ok, i - 1)
                    nc.vector.tensor_scalar(xn[:, i % 2], xt[:, i % 3], rstd[:, i:i + 1], None, ALU.mult).then_inc(scaled, 1)
                if i >= 1:
                    j = i - 1
                    dve.wait_ge(turned_ok, j + 1)
                    if j >= 2:
                        dve.wait_ge(stored[j % 2], 16 * (j // 2))
                    nc.vector.tensor_copy(outT[:, j % 2], turned[:, j % 2].rearrange("p a b -> p (a b)")).then_inc(copied, 1)

        @block.tensor
        def _(pe):
            pe.wait_ge(ident_ok, 2)
            for i in range(NT):
                pe.wait_ge(scaled, i + 1)
                if i >= 2:
                    pe.wait_ge(copied, i - 1)
                for k in range(KC):
                    ins = nc.tensor.transpose(turned[:, i % 2, k // 4, (k % 4) * P:(k % 4 + 1) * P],
                                              xn[:, i % 2, k * P:(k + 1) * P], ident[:, :])
                ins.then_inc(turned_ok, 1)


class Modulated:

    def __init__(self, st, s_xnT, s_mod, gain, shift_at, scale_at, scratch):
        self.st, self.nc = st, st.nc
        self.src, self.mod, self.gain, self.shift_at, self.scale_at = s_xnT, s_mod, gain, shift_at, scale_at
        self.high = st.sb("h_high", [P, KC, SEQ], F32R)
        self.low = st.sb("h_low", [P, KC, SEQ], F32R)
        self.cols = st.sb("mod_cols", [P, 3, KC])
        self.slots = scratch
        self.cols_in = st.sem("cols_in")
        self.x_in = [st.sem(f"xb_in{s}") for s in range(4)]
        self.made, self.step = st.sem("h_made"), st.sem("h_step")

    def load(self, sp):
        sp.dma_start(self.cols[:, 0], self.gain).then_inc(self.cols_in, 16)
        for n, at in ((1, self.scale_at), (2, self.shift_at)):
            sp.dma_start(self.cols[:, n], self.mod[0, at:at + D].rearrange("(k p) -> p k", p=P),
                         allow_slow_non_contiguous=True).then_inc(self.cols_in, 16)
        for m in range(NB * KC):
            n, k = m // KC, m % KC
            if m >= 4:
                sp.wait_ge(self.made, m - 3)
            sp.dma_start(self.slots[:, m % 4], self.src[k * P:(k + 1) * P, n * BLK:(n + 1) * BLK])\
              .then_inc(self.x_in[m % 4], 16)

    def make(self, dve):
        v = self.nc.vector
        steps = Steps(dve, self.step)
        dve.wait_ge(self.cols_in, 48)
        steps.did(v.tensor_scalar(self.cols[:, 1], self.cols[:, 1], 1.0, None, ALU.add))
        steps.wait()
        steps.did(v.tensor_tensor(self.cols[:, 0], self.cols[:, 0], self.cols[:, 1], ALU.mult))
        steps.wait()
        for m in range(NB * KC):
            n, k = m // KC, m % KC
            x = self.slots[:, m % 4]
            high, low = (t[:, k, n * BLK:(n + 1) * BLK] for t in (self.high, self.low))
            dve.wait_ge(self.x_in[m % 4], 16 * (m // 4 + 1))
            steps.did(v.tensor_scalar(x, x, self.cols[:, 0, k:k + 1], self.cols[:, 2, k:k + 1], ALU.mult, ALU.add))
            steps.wait()
            steps.did(v.tensor_copy(high, x))
            steps.wait()
            v.tensor_tensor(low, x, high.bitcast(F32), ALU.subtract).then_inc(self.made, 1)


def three_passes(nc, out, w_high, w_low, h_high, h_low):
    for k in range(KC):
        nc.tensor.matmul(out, w_high[:, k], h_high[:, k], start=k == 0, stop=False)
        nc.tensor.matmul(out, w_high[:, k], h_low[:, k], start=False, stop=False)
        ins = nc.tensor.matmul(out, w_low[:, k], h_high[:, k], start=False, stop=k == KC - 1)
    return ins


def deltanet_projection(nc, s_xnT, s_mod, a_pre_g, a_w_in, a_conv_w, s_qkv, s_zT, s_abT):
    TPI = 4
    PER = TPI * NB
    QK_ITERS, V_ITERS, Z_ITERS = 2 * AH // TPI, AH // TPI, AH // TPI
    ITERS = QK_ITERS + V_ITERS + Z_ITERS
    with Stage(nc, "pa") as st:
        ybuf = st.sb("ybuf", [P, 2, 3 + SEQ])
        acc = st.sb("acc", [P, SEQ])
        sil = st.sb("sil", [P, SEQ])
        sq = st.sb("sq", [P, SEQ])
        h = Modulated(st, s_xnT, s_mod, a_pre_g, 0, D, sq[:, :].rearrange("p (s t) -> p s t", s=4))
        wraw = st.sb("wraw", [P, KC, TPI * P])
        w_high = st.sb("w_high", [P, 2, KC, P], F32R)
        w_low = st.sb("w_low", [P, 2, KC, P], F32R)
        wab = st.sb("wab", [P, KC, 2 * AH])
        taps = st.sb("taps", [P, 3 * AH, 4])
        ones = st.sb("ones", [P, P])
        eps = st.sb("eps", [P, 1])
        y = st.ps("y", [P, NB, BLK])
        norm = st.ps("norm", [P, NB, BLK])
        taps_in, w_in, ab_in = st.sem("taps_in"), st.sem("w_in"), st.sem("ab_in")
        consts_set = st.sem("consts_set")
        w_split, bank_full, bank_free = st.sem("w_split"), st.sem("bank_full"), st.sem("bank_free")
        convolved, silu_done, squared = st.sem("convolved"), st.sem("silu_done"), st.sem("squared")
        summed, rooted, scaled, stored = st.sem("summed"), st.sem("rooted"), st.sem("scaled"), st.pool_sem("stored")
        dve_step, act_step = st.sem("dve_step"), st.sem("act_step")
        block = st.block()

        def weights(i):
            return a_w_in[:, bass.ds(i * (TPI * P), TPI * P)].rearrange("(k p) f -> p k f", p=P)

        @block.sync
        def _(sp):
            sp.dma_start(wraw[:, :, :], weights(0)).then_inc(w_in, 16)
            h.load(sp)
            sp.dma_start(taps[:, :, :], a_conv_w).then_inc(taps_in, 16)
            sp.dma_start(wab[:, :, :], a_w_in[:, 4 * D:4 * D + 2 * AH].rearrange("(k p) f -> p k f", p=P))\
              .then_inc(ab_in, 16)
            with sp.Fori(1, ITERS) as i:
                sp.wait_ge(w_split, i * TPI)
                sp.dma_start(wraw[:, :, :], weights(i)).then_inc(w_in, 16)

        def tensor_tile(pe, T, slot, norm_before):
            pe.wait_ge(w_split, T + 1)
            for n in range(NB):
                pe.wait_ge(h.made, (n + 1) * KC)
                pe.wait_ge(bank_free, T * NB + (n + 1))
                three_passes(nc, y[:, n], w_high[:, slot], w_low[:, slot], h.high[:, :, n * BLK:(n + 1) * BLK],
                             h.low[:, :, n * BLK:(n + 1) * BLK]).then_inc(bank_full, 1)
            if norm_before:
                pe.wait_ge(squared, T + 1)
                for n in range(NB):
                    ins = nc.tensor.matmul(norm[:, n], ones[:, :], sq[:, n * BLK:(n + 1) * BLK], start=True, stop=True)
                ins.then_inc(summed, 1)

        @block.tensor
        def _(pe):
            pe.wait_ge(consts_set, 1)
            with pe.Fori(0, QK_ITERS) as i:
                for t in range(TPI):
                    tensor_tile(pe, i * TPI + t, t % 2, True)
            for T in range(QK_ITERS * TPI, ITERS * TPI + 1):
                tensor_tile(pe, T, T % 2, T == QK_ITERS * TPI)

        def split(dve, slot, raw, steps):
            steps.did(nc.vector.tensor_copy(w_high[:, slot, :, 0:raw.shape[2]], raw))
            steps.wait()
            nc.vector.tensor_tensor(w_low[:, slot, :, 0:raw.shape[2]], raw,
                                    w_high[:, slot, :, 0:raw.shape[2]].bitcast(F32), ALU.subtract).then_inc(w_split, 1)

        def vector_tile(dve, i, T, t, norm_before, convolve, steps):
            dve.wait_ge(bank_full, T * NB + NB)
            if t == 0:
                dve.wait_ge(w_in, (i + 1) * 16)
            if t == 2:
                dve.wait_ge(w_in, (i + 2) * 16)
            at = (t + 2) % TPI * P
            split(dve, t % 2, wraw[:, :, at:at + P], steps)
            post(dve, T, t % 2, norm_before, convolve, steps)

        def post(dve, T, slot, norm_before, convolve, steps):
            if norm_before:
                dve.wait_ge(rooted, T + 1)
                nc.vector.tensor_tensor(sil[:, :], sil[:, :], sq[:, :], ALU.mult).then_inc(scaled, 1)
            if convolve:
                dve.wait_ge(bank_free, T * NB + 2 * NB)
                dve.wait_ge(silu_done, T + 1)
                for j in range(4):
                    x = ybuf[:, slot, j:j + SEQ]
                    w = taps[:, bass.ds(T, 1), j:j + 1].rearrange("p a b -> p (a b)")
                    if j == 0:
                        steps.did(nc.vector.tensor_scalar(acc[:, :], x, w, None, ALU.mult))
                        continue
                    steps.wait()
                    ins = nc.vector.scalar_tensor_tensor(acc[:, :], x, w, acc[:, :], ALU.mult, ALU.add)
                    steps.did(ins) if j < 3 else ins.then_inc(convolved, 1)

        @block.vector
        def _(dve):
            nc.vector.memset(ones[:, :], 1.0).then_inc(consts_set, 1)
            nc.vector.memset(sil[:, :], 0.0)
            nc.vector.memset(eps[:, :], EPS)
            nc.vector.memset(ybuf[:, :, 0:3], 0.0).then_inc(dve_step, 1)
            dve.wait_ge(dve_step, 1)
            for s, credit in ((bank_free, NB), (convolved, 2), (silu_done, 1)):
                dve.sem_inc(s, credit)
            steps = Steps(dve, dve_step)
            steps.n = 1
            dve.wait_ge(w_in, 16)
            for T in range(2):
                split(dve, T, wraw[:, :, T * P:(T + 1) * P], steps)
            h.make(dve)
            dve.wait_ge(h.made, NB * KC)
            nc.vector.memset(sq[:, :], 1.0).then_inc(squared, 1)
            start = steps.n
            dve.wait_ge(taps_in, 16)
            with dve.Fori(0, QK_ITERS) as i:
                PER_ITER = TPI * 4
                steps.restart(i * PER_ITER + start)
                for t in range(TPI):
                    vector_tile(dve, i, i * TPI + t, t, True, True, steps)
                assert steps.n == PER_ITER
            steps.restart(QK_ITERS * PER_ITER + start)
            for T in range(QK_ITERS * TPI, ITERS * TPI):
                i, t = T // TPI, T % TPI
                convolve = i < QK_ITERS + V_ITERS
                if i < ITERS - 1 or t < 2:
                    vector_tile(dve, i, T, t, T == QK_ITERS * TPI, convolve, steps)
                elif t == 2:
                    dve.wait_ge(bank_full, T * NB + NB)
                    dve.wait_ge(ab_in, 16)
                    steps.did(nc.vector.memset(w_high[:, 0].bitcast(F32), 0.0))
                    steps.did(nc.vector.memset(w_low[:, 0].bitcast(F32), 0.0))
                    steps.wait()
                    split(dve, 0, wab[:, :, :], steps)
                    

        def scalar_tile(act, T, slot, norm_before, kind, steps):
            if kind == "z":
                act.wait_ge(stored, 16 * (T + 1))
            elif kind != "ab":
                act.wait_ge(convolved, T + 1)
            for n in range(NB):
                act.wait_ge(bank_full, T * NB + (n + 1))
                out, f, rows = {"z": (sil[:, n * BLK:(n + 1) * BLK], ACT.Silu, P),
                                "ab": (acc[0:2 * AH, n * BLK:(n + 1) * BLK], ACT.Copy, 2 * AH)}\
                    .get(kind, (ybuf[:, slot, 3 + n * BLK:3 + (n + 1) * BLK], ACT.Copy, P))
                nc.scalar.activation(out, y[0:rows, n], f).then_inc(bank_free, 1)
            if norm_before:
                act.wait_ge(summed, T + 1)
                steps.did(nc.scalar.activation(sq[:, :], norm[:, :].rearrange("p a b -> p (a b)"), ACT.Ln, bias=eps[:, :]))
                steps.wait()
                nc.scalar.activation(sq[:, :], sq[:, :], ACT.Exp, scale=-0.5).then_inc(rooted, 1)
            if kind in ("z", "ab"):
                return
            act.wait_ge(convolved, T + 3)
            act.wait_ge(stored, 16 * (T + 1))
            nc.scalar.activation(sil[:, :], acc[:, :], ACT.Silu).then_inc(silu_done, 1)
            if kind == "qk":
                act.wait_ge(silu_done, T + 2)
                act.wait_ge(scaled, T + 1)
                nc.scalar.activation(sq[:, :], sil[:, :], ACT.Square).then_inc(squared, 1)

        @block.scalar
        def _(act):
            steps = Steps(act, act_step)
            act.wait_ge(dve_step, 1)
            with act.Fori(0, QK_ITERS) as i:
                steps.restart(i * TPI)
                for t in range(TPI):
                    scalar_tile(act, i * TPI + t, t % 2, True, "qk", steps)
            steps.restart(QK_ITERS * TPI)
            for T in range(QK_ITERS * TPI, ITERS * TPI + 1):
                kind = "v" if T < (QK_ITERS + V_ITERS) * TPI else "z" if T < ITERS * TPI else "ab"
                if kind == "ab":
                    act.wait_ge(silu_done, (QK_ITERS + V_ITERS) * TPI + 1)
                scalar_tile(act, T, T % 2, T == QK_ITERS * TPI, kind, steps)

        @block.gpsimd
        def _(pool):
            with pool.Fori(0, QK_ITERS * TPI) as T:
                pool.wait_ge(scaled, T + 1)
                pool.dma_start(s_qkv[bass.ds(T * P, P), :], sil[:, :]).then_inc(stored, 16)
            T = QK_ITERS * TPI
            pool.wait_ge(scaled, T + 1)
            pool.dma_start(s_qkv[T * P:(T + 1) * P, :], sil[:, :]).then_inc(stored, 16)
            for T in range(QK_ITERS * TPI, (QK_ITERS + V_ITERS) * TPI):
                pool.wait_ge(silu_done, T + 2)
                pool.dma_start(s_qkv[(T + 1) * P:(T + 2) * P, :], sil[:, :]).then_inc(stored, 16)
            for T in range((QK_ITERS + V_ITERS) * TPI, ITERS * TPI):
                pool.wait_ge(bank_free, (T + 2) * NB)
                at = (T - (QK_ITERS + V_ITERS) * TPI) * P
                pool.dma_start(s_zT[at:at + P, :], sil[:, :]).then_inc(stored, 16)
            pool.wait_ge(bank_free, (ITERS * TPI + 2) * NB)
            pool.dma_start(s_abT[:, :], acc[0:2 * AH, :]).then_inc(stored, 16)
            pool.wait_ge(stored, 16 * (ITERS * TPI + 2))


class Event:

    def __init__(self, st, name, per=2, credit=0):
        self.sem, self.per, self.credit = st.sem(name), per, credit

    def wait(self, eng, rnd, part, back=0):
        value = rnd * self.per + (part + 1 + self.credit - back * self.per)
        assert not isinstance(value, int) or value > 0
        eng.wait_ge(self.sem, value)

    def done(self, ins):
        return ins.then_inc(self.sem, 1)

    def give_credit(self, eng):
        if self.credit:
            eng.sem_inc(self.sem, self.credit)


def over_heads(mask, n):
    return mask.unsqueeze(1).to_broadcast([P, n, P])


def delta_rule(nc, s_qkv, s_zT, s_abT, a_log, dt_bias, o_gain, level_masks, s_g, s_uT):
    C = P
    NC = SEQ // C
    HG = AH // 2
    LV = 7
    G_, GB_, BETA, NBEG, EKG, EGL = range(6)
    SCALE = float(P) ** -0.5
    with Stage(nc, "dr") as st:
        araw, braw = st.sb("araw", [AH, SEQ]), st.sb("braw", [AH, SEQ])
        atmp, btmp = st.sb("atmp", [AH, SEQ]), st.sb("btmp", [AH, SEQ])
        keep = st.sb("keep", [AH, SEQ])
        hcol = st.sb("hcol", [AH, 4])
        cols = st.sb("cols", [P, 6, NC, AH])
        ident, last_row = st.sb("ident", [P, P]), st.sb("last_row", [P, P])
        eps = st.sb("eps", [P, 1])
        gain = st.sb("gain", [P, 1])
        mask_a, mask_p = st.sb("mask_a", [P, P]), st.sb("mask_p", [P, P])
        levels = st.sb("levels", [P, 2, LV, P], U8)
        qkv = [st.sb(f"qkv{s}", [P, 3 * AH, C]) for s in range(2)]
        z = [st.sb(f"z{s}", [P, AH, C]) for s in range(2)]
        gb = [st.sb(f"gb{s}", [P, AH, C]) for s in range(2)]
        arg_a, arg_p = st.sb("arg_a", [P, AH, C]), st.sb("arg_p", [P, AH, C])
        sd, sa = st.sb("sd", [P, 6, AH]), st.sb("sa", [P, 6, AH])
        q_hat, bv, k_hat = (st.sb(n, [P, AH, C]) for n in ("q_hat", "bv", "k_hat"))
        B, PT, T, TT, Z = (st.sb(n, [P, AH, C]) for n in ("B", "PT", "T", "TT", "Z"))
        R, VN, S, ON, U = (st.sb(n, [P, AH, C]) for n in ("R", "VN", "S", "ON", "U"))
        ss, rstd = st.sb("ss", [P, AH]), st.sb("rstd", [P, AH])
        psX, psZ, psT, psTT = (st.ps(n, [P, 2, BLK]) for n in ("psX", "psZ", "psT", "psTT"))

        consts_in, levels_set, ab_in = st.sem("consts_in"), st.sem("levels_set"), st.sem("ab_in")
        pool_set, dve_gates, act_gates, gates_stored = (st.sem(n) for n in ("pool_set", "dve_gates", "act_gates", "gates_stored"))
        turned, tables = st.sem("turned"), st.sem("tables")
        qkv_in, z_in, gb_in = ([st.sem(f"{n}{s}") for s in range(2)] for n in ("qkv_in", "z_in", "gb_in"))
        stored = [st.sem(f"stored{g}") for g in range(2)]
        dve_passed, pool_passed = st.sem("dve_passed"), st.sem("pool_passed")
        ev = lambda name, per=2, credit=0: Event(st, name, per, credit)
        scal_d, scal_a = ev("scal_d", 1), ev("scal_a", 1)
        args, decays, qh_ok, bv_ok, kh_ok = ev("args"), ev("decays"), ev("qh_ok"), ev("bv_ok"), ev("kh_ok")
        v_turned, k_turned, gram_ok, qk_ok = ev("v_turned"), ev("k_turned"), ev("gram_ok"), ev("qk_ok")
        b_ok, pt_ok = ev("b_ok"), ev("pt_ok")
        reset, z_ok, z_copied = ev("reset"), ev("z_ok", 2 * LV), ev("z_copied", 2 * (LV - 1))
        t_ok, level_ok = ev("t_ok", 2 * (LV - 1)), ev("level_ok", 2 * LV, credit=0)
        ks_ok, r_ok, tr_ok, vn_ok = ev("ks_ok"), ev("r_ok"), ev("tr_ok", credit=2), ev("vn_ok", credit=2)
        o_ok, st_ok, s_ok, squares, on_ok = ev("o_ok", credit=2), ev("st_ok"), ev("s_ok", credit=2), ev("squares"), ev("on_ok", credit=2)
        norm_step = ev("norm_step", 4)
        ot_ok, out_ok = ev("ot_ok", credit=2), ev("out_ok", credit=2)
        block = st.block()

        def group(g):
            return slice(g * HG, (g + 1) * HG)

        def flat(x, g):
            return x[:, group(g)].rearrange("p h c -> p (h c)")

        def heads(g):
            return range(g * HG, (g + 1) * HG)

        def at(ps, g, h):
            return ps[:, g, (h % HG) * C:(h % HG + 1) * C]

        def load(sp, c, s):
            tok = bass.ds(c * C, C)
            sp.dma_start(gb[s][:, :, :], s_g[:, tok].unsqueeze(0).to_broadcast([P, AH, C])).then_inc(gb_in[s], 16)
            sp.dma_start(qkv[s][:, :, :], s_qkv[P:, tok].rearrange("(t p) s -> p t s", p=P)).then_inc(qkv_in[s], 16)
            sp.dma_start(z[s][:, :, :], s_zT[:, tok].rearrange("(t p) s -> p t s", p=P)).then_inc(z_in[s], 16)

        def store(sp, c):
            for g in range(2):
                out_ok.wait(sp, c, g)
                sp.dma_start(s_uT[g * HG * P:(g + 1) * HG * P, bass.ds(c * C, C)].rearrange("(h p) s -> p h s", p=P),
                             U[:, group(g)]).then_inc(stored[g], 16)

        @block.sync
        def _(sp):
            sp.dma_start(araw[:, :], s_abT[0:AH, :]).then_inc(ab_in, 16)
            sp.dma_start(braw[:, :], s_abT[AH:2 * AH, :]).then_inc(ab_in, 16)
            sp.dma_start(hcol[:, 0:1], a_log).then_inc(ab_in, 16)
            sp.dma_start(hcol[:, 1:2], dt_bias).then_inc(ab_in, 16)
            sp.dma_start(gain[:, :], o_gain).then_inc(consts_in, 16)
            for n, x in enumerate((B, Z)):
                sp.dma_start(x[:, 0:LV], level_masks[:, n]).then_inc(consts_in, 16)
            sp.wait_ge(dve_gates, 6)
            sp.dma_start(s_g[:, :], araw[:, :]).then_inc(gates_stored, 16)
            sp.wait_ge(gates_stored, 16)
            for s in range(2):
                load(sp, s, s)
            for g in range(2):
                sp.sem_inc(stored[g], 16)
            with sp.Fori(0, NC // 2 - 1) as i:
                for s in range(2):
                    store(sp, i * 2 + s)
                    load(sp, i * 2 + (s + 2), s)
            for c in range(NC - 2, NC):
                store(sp, c)
            for g in range(2):
                sp.wait_ge(stored[g], 16 * (NC + 1))

        @block.gpsimd
        def _(pool):
            g = nc.gpsimd
            g.memset(ident[:, :], 0.0)
            g.memset(last_row[:, :], 0.0)
            g.memset(keep[:, :], 1.0)
            g.memset(eps[:, :], EPS)
            g.memset(mask_a[:, :], 0.0)
            g.memset(S[:, :, :], 0.0)
            g.memset(mask_p[:, :], 0.0).then_inc(pool_set, 1)
            pool.wait_ge(pool_set, 1)
            sel = lambda x, fill, op, base, step, mult: g.affine_select(
                out=x, in_=x, compare_op=op, fill=fill, base=base, pattern=[[step, P]], channel_multiplier=mult)
            sel(ident[:, :], 1.0, ALU.not_equal, 0, -1, 1)
            g.affine_select(out=last_row[:, :], in_=last_row[:, :], compare_op=ALU.not_equal, fill=1.0,
                            base=-(P - 1), pattern=[[0, P]], channel_multiplier=1)
            sel(mask_a[:, :], BIG, ALU.is_gt, 0, -1, 1)
            sel(mask_p[:, :], -BIG, ALU.is_ge, 0, 1, -1)
            g.memset(keep[:, 0:SEQ:C], 0.0).then_inc(pool_set, 1)
            for e in (tr_ok, vn_ok, s_ok, o_ok, on_ok, ot_ok, out_ok):
                e.give_credit(pool)
            pool.wait_ge(pool_set, 2)
            with pool.Fori(0, NC) as c:
                for q in range(2):
                    tr_ok.wait(pool, c, q, back=1)
                    pool.sem_inc(pool_passed, 1)
                    for h in heads(q):
                        g.tensor_copy(T[:, h], ident[:, :])
                        ins = g.tensor_copy(TT[:, h], ident[:, :])
                    reset.done(ins)

        def gates_vector(dve):
            v = nc.vector
            steps = Steps(dve, dve_gates)
            dve.wait_ge(ab_in, 64)
            dve.wait_ge(pool_set, 2)
            steps.did(v.tensor_scalar(araw[:, :], araw[:, :], hcol[:, 1:2], None, ALU.add))
            steps.wait()
            steps.did(v.scalar_tensor_tensor(atmp[:, :], araw[:, :], -1.0, araw[:, :], ALU.mult, ALU.max))
            steps.did(v.scalar_tensor_tensor(btmp[:, :], braw[:, :], -1.0, braw[:, :], ALU.mult, ALU.max))
            dve.wait_ge(act_gates, 5)
            steps.did(v.scalar_tensor_tensor(atmp[:, :], araw[:, :], 0.0, atmp[:, :], ALU.max, ALU.add))
            steps.wait()
            steps.did(v.tensor_scalar(atmp[:, :], atmp[:, :], hcol[:, 2:3], -1.0, ALU.mult, ALU.mult))
            steps.wait()
            steps.did(v.tensor_tensor_scan(araw[:, :], keep[:, :], atmp[:, :], 0.0, ALU.mult, ALU.add))
            steps.did(v.scalar_tensor_tensor(btmp[:, :], braw[:, :], 0.0, btmp[:, :], ALU.min, ALU.subtract))
            dve.wait_ge(turned, 1)
            raw = psX[:, 0].rearrange("p (k c h) -> p k c h", k=4, h=AH)
            n = steps.n
            steps.did(v.tensor_copy(cols[:, G_], raw[:, 0]))
            steps.wait()
            steps.did(v.tensor_tensor(cols[:, GB_], raw[:, 1], cols[:, G_], ALU.add))
            steps.did(v.tensor_copy(cols[:, BETA], raw[:, 1]))
            dve.wait_ge(turned, 2)
            steps.did(v.tensor_tensor(cols[:, EKG], psX[:, 1, 0:NC * AH].rearrange("p (c h) -> p c h", h=AH), cols[:, G_], ALU.subtract))
            steps.did(v.tensor_copy(cols[:, EGL], psX[:, 1, 0:NC * AH].rearrange("p (c h) -> p c h", h=AH)))
            steps.wait()
            dve.sem_inc(tables, 1)
            dve.wait_ge(act_gates, 9)
            steps.did(v.tensor_scalar(cols[:, NBEG], cols[:, NBEG], -1.0, None, ALU.mult))
            steps.wait()
            dve.sem_inc(tables, 1)

        def gates_scalar(act):
            a = nc.scalar
            steps = Steps(act, act_gates)
            act.wait_ge(ab_in, 64)
            act.wait_ge(pool_set, 2)
            steps.did(a.activation(hcol[:, 2:3], hcol[:, 0:1], ACT.Exp))
            act.wait_ge(dve_gates, 3)
            for x in (atmp, btmp):
                steps.did(a.activation(x[:, :], x[:, :], ACT.Exp, scale=-1.0))
                steps.wait()
                steps.did(a.activation(x[:, :], x[:, :], ACT.Ln, bias=1.0))
            act.wait_ge(tables, 1)
            steps.did(a.activation(cols[:, NBEG], cols[:, GB_], ACT.Exp))
            for k in (BETA, EKG, EGL):
                steps.did(a.activation(cols[:, k], cols[:, k], ACT.Exp))
            act.wait_ge(tables, 2)

        def gates_tensor(pe):
            pe.wait_ge(pool_set, 2)
            pe.wait_ge(dve_gates, 7)
            raw = psX[:, 0].rearrange("p (k c h) -> p k c h", k=4, h=AH)
            for k, x in ((0, araw), (1, btmp)):
                for c in range(NC):
                    ins = nc.tensor.transpose(raw[:, k, c], x[:, c * C:(c + 1) * C], ident[0:AH, 0:AH])
            ins.then_inc(turned, 1)
            pe.wait_ge(dve_gates, 8)
            nc.tensor.matmul(psX[:, 1, 0:NC * AH], last_row[:, :], cols[:, G_].rearrange("p c h -> p (c h)"),
                             start=True, stop=True).then_inc(turned, 1)
            pe.wait_ge(tables, 2)

        def tensor_chunk(pe, c, i, s):
            mm, tr = nc.tensor.matmul, nc.tensor.transpose
            q, k, v = (qkv[s][:, j * AH:(j + 1) * AH] for j in range(3))
            pe.wait_ge(qkv_in[s], i * 16 + 16)
            for g in range(2):
                vn_ok.wait(pe, c, g, back=1)
                for h in heads(g):
                    ins = tr(at(psZ, g, h), v[:, h], ident[:, :])
                v_turned.done(ins)
                out_ok.wait(pe, c, g, back=1)
                for h in heads(g):
                    ins = tr(at(psX, g, h), k[:, h], ident[:, :])
                k_turned.done(ins)
                on_ok.wait(pe, c, g, back=1)
                for h in heads(g):
                    ins = mm(at(psT, g, h), k[:, h], k[:, h], start=True, stop=True)
                gram_ok.done(ins)
                s_ok.wait(pe, c, g, back=1)
                for h in heads(g):
                    ins = mm(at(psTT, g, h), k[:, h], q[:, h], start=True, stop=True)
                qk_ok.done(ins)
            for g in range(2):
                b_ok.wait(pe, c, g)
                bv_ok.wait(pe, c, g)
                for h in heads(g):
                    ins = tr(at(psZ, g, h), B[:, h], ident[:, :])
                z_ok.done(ins)
            for l in range(1, LV):
                for g in range(2):
                    level_ok.wait(pe, c, 2 * (l - 1) + g)
                    for h in heads(g):
                        ins = mm(at(psZ, g, h), B[:, h], TT[:, h], start=True, stop=True)
                    z_ok.done(ins)
                for g in range(2):
                    z_copied.wait(pe, c, 2 * (l - 1) + g)
                    if l < LV - 1:
                        for h in heads(g):
                            mm(at(psT, g, h), Z[:, h], T[:, h], start=True, stop=True)
                    for h in heads(g):
                        ins = mm(at(psTT, g, h), T[:, h], Z[:, h], start=True, stop=True)
                    t_ok.done(ins)
            for g in range(2):
                kh_ok.wait(pe, c, g)
                for h in heads(g):
                    ins = mm(at(psX, g, h), k[:, h], S[:, h], start=True, stop=True)
                ks_ok.done(ins)
            for g in range(2):
                level_ok.wait(pe, c, 2 * (LV - 1) + g)
                r_ok.wait(pe, c, g)
                for h in heads(g):
                    ins = mm(at(psZ, g, h), TT[:, h], R[:, h], start=True, stop=True)
                tr_ok.done(ins)
            for g in range(2):
                qh_ok.wait(pe, c, g)
                vn_ok.wait(pe, c, g)
                for h in heads(g):
                    mm(at(psT, g, h), q_hat[:, h], S[:, h], start=True, stop=False)
                    ins = mm(at(psT, g, h), PT[:, h], VN[:, h], start=False, stop=True)
                o_ok.done(ins)
                for h in heads(g):
                    ins = mm(at(psTT, g, h), k_hat[:, h], VN[:, h], start=True, stop=True)
                st_ok.done(ins)
            for g in range(2):
                on_ok.wait(pe, c, g)
                for h in heads(g):
                    ins = tr(at(psX, g, h), ON[:, h], ident[:, :])
                ot_ok.done(ins)

        def vector_chunk(dve, c, i, s):
            v = nc.vector
            stt = v.scalar_tensor_tensor
            q = qkv[s][:, 0:AH]
            s_ok.wait(dve, c, 1, back=1)
            scal_d.done(v.tensor_copy(sd[:, :, :], cols[:, :, bass.ds(c, 1)].rearrange("p k a h -> p k (a h)")))
            scal_d.wait(dve, c, 0)
            dve.wait_ge(gb_in[s], i * 16 + 16)
            for g in range(2):
                for h in heads(g):
                    stt(arg_a[:, h], gb[s][:, h], sd[:, GB_, h:h + 1], mask_a[:, :], ALU.subtract, ALU.add)
                    ins = stt(arg_p[:, h], gb[s][:, h], sd[:, G_, h:h + 1], mask_p[:, :], ALU.subtract, ALU.add)
                args.done(ins)
            dve.wait_ge(qkv_in[s], i * 16 + 16)
            for g in range(2):
                decays.wait(dve, c, g)
                o_ok.wait(dve, c, g, back=1)
                qh_ok.done(stt(flat(q_hat, g), flat(q, g), SCALE, flat(gb[s], g), ALU.mult, ALU.mult))
            for g in range(2):
                v_turned.wait(dve, c, g)
                for h in heads(g):
                    ins = v.tensor_scalar(bv[:, h], at(psZ, g, h), sd[:, BETA, h:h + 1], None, ALU.mult)
                bv_ok.done(ins)
                gram_ok.wait(dve, c, g)
                b_ok.done(stt(flat(B, g), psT[:, g], -1.0, flat(arg_a, g), ALU.mult, ALU.mult))
                qk_ok.wait(dve, c, g)
                pt_ok.done(stt(flat(PT, g), psTT[:, g], SCALE, flat(arg_p, g), ALU.mult, ALU.mult))
            for g in range(2):
                z_ok.wait(dve, c, g)
                reset.wait(dve, c, g)
                b_ok.wait(dve, c, g)
                dve.sem_inc(dve_passed, 1)
                v.copy_predicated(T[:, group(g)], over_heads(levels[:, 0, 0], HG), B[:, group(g)])
                level_ok.done(v.copy_predicated(TT[:, group(g)], over_heads(levels[:, 1, 0], HG),
                                                psZ[:, g].rearrange("p (h c) -> p h c", h=HG)))
            for l in range(1, LV):
                for g in range(2):
                    t_ok.wait(dve, c, 2 * (l - 1) + g)
                    level_ok.wait(dve, c, 2 * (l - 1) + g)
                    dve.sem_inc(dve_passed, 1)
                    if l < LV - 1:
                        v.copy_predicated(T[:, group(g)], over_heads(levels[:, 0, l], HG),
                                          psT[:, g].rearrange("p (h c) -> p h c", h=HG))
                    level_ok.done(v.copy_predicated(TT[:, group(g)], over_heads(levels[:, 1, l], HG),
                                                    psTT[:, g].rearrange("p (h c) -> p h c", h=HG)))
            for g in range(2):
                ks_ok.wait(dve, c, g)
                bv_ok.wait(dve, c, g)
                for h in heads(g):
                    ins = stt(R[:, h], at(psX, g, h), sd[:, NBEG, h:h + 1], bv[:, h], ALU.mult, ALU.add)
                r_ok.done(ins)
            for g in range(2):
                st_ok.wait(dve, c, g)
                s_ok.wait(dve, c, g, back=1)
                for h in heads(g):
                    ins = stt(S[:, h], S[:, h], sd[:, EGL, h:h + 1], at(psTT, g, h), ALU.mult, ALU.add)
                s_ok.done(ins)
            dve.wait_ge(z_in[s], i * 16 + 16)
            for g in range(2):
                ot_ok.wait(dve, c, g)
                dve.wait_ge(stored[g], c * 16 + 16)
                out_ok.done(stt(flat(U, g), psX[:, g], gain[:, 0:1], flat(z[s], g), ALU.mult, ALU.mult))

        def scalar_chunk(act, c, i, s):
            a = nc.scalar
            on_ok.wait(act, c, 1, back=1)
            scal_a.done(a.activation(sa[:, :, :], cols[:, :, bass.ds(c, 1)].rearrange("p k a h -> p k (a h)"), ACT.Copy))
            for g in range(2):
                args.wait(act, c, g)
                act.wait_ge(gb_in[s], i * 16 + 16)
                a.activation(flat(arg_a, g), flat(arg_a, g), ACT.Exp, scale=-1.0)
                a.activation(flat(arg_p, g), flat(arg_p, g), ACT.Exp)
                decays.done(a.activation(flat(gb[s], g), flat(gb[s], g), ACT.Exp))
            scal_a.wait(act, c, 0)
            for g in range(2):
                k_turned.wait(act, c, g)
                for h in heads(g):
                    ins = a.activation(k_hat[:, h], at(psX, g, h), ACT.Copy, scale=sa[:, EKG, h:h + 1])
                kh_ok.done(ins)
            for l in range(1, LV):
                for g in range(2):
                    z_ok.wait(act, c, 2 * l + g)
                    z_copied.done(a.activation(flat(Z, g), psZ[:, g], ACT.Copy))
            for g in range(2):
                tr_ok.wait(act, c, g)
                vn_ok.done(a.activation(flat(VN, g), psZ[:, g], ACT.Copy))
            for g in range(2):
                o_ok.wait(act, c, g)
                for h in heads(g):
                    ins = a.activation(ON[:, h], at(psT, g, h), ACT.Square, accum_out=ss[:, h:h + 1])
                squares.done(ins)
                squares.wait(act, c, g)
                norm_step.done(a.activation(ss[:, group(g)], ss[:, group(g)], ACT.Ln, bias=eps[:, :], scale=1.0 / P))
                norm_step.wait(act, c, 2 * g)
                norm_step.done(a.activation(rstd[:, group(g)], ss[:, group(g)], ACT.Exp, scale=-0.5))
                norm_step.wait(act, c, 2 * g + 1)
                for h in heads(g):
                    ins = a.activation(ON[:, h], at(psT, g, h), ACT.Copy, scale=rstd[:, h:h + 1])
                on_ok.done(ins)

        @block.tensor
        def _(pe):
            gates_tensor(pe)
            with pe.Fori(0, NC // 2) as i:
                for s in range(2):
                    tensor_chunk(pe, i * 2 + s, i, s)

        @block.vector
        def _(dve):
            gates_vector(dve)
            dve.wait_ge(consts_in, 48)
            for n, x in enumerate((B, Z)):
                nc.vector.tensor_copy(levels[:, n], x[:, 0:LV]).then_inc(levels_set, 1)
            dve.wait_ge(levels_set, 2)
            with dve.Fori(0, NC // 2) as i:
                for s in range(2):
                    vector_chunk(dve, i * 2 + s, i, s)

        @block.scalar
        def _(act):
            gates_scalar(act)
            with act.Fori(0, NC // 2) as i:
                for s in range(2):
                    scalar_chunk(act, i * 2 + s, i, s)


def output_projection(nc, name, s_uT, w_out, s_mod, gate_at, post_g, x, x_out, s_xnT):
    with Stage(nc, name) as st:
        ident, eps = st.sb("ident", [P, P]), st.sb("eps", [P, 1])
        w_high, w_low = st.sb("w_high", [P, KC, D], F32R), st.sb("w_low", [P, KC, D], F32R)
        wraw = st.sb("wraw", [P, 2, D])
        gate, post = st.sb("gate", [P, D]), st.sb("post", [P, D])
        u = st.sb("u", [P, 2, KC, P])
        u_high, u_low = st.sb("u_high", [P, 2, KC, P], F32R), st.sb("u_low", [P, 2, KC, P], F32R)
        xt, xo, xn, xT = (st.sb(n, [P, 2, D]) for n in ("xt", "xo", "xn", "xT"))
        junk = st.sb("junk", [P, 2, D])
        ss = st.sb("ss", [P, 4, 1])
        y, turned = st.ps("y", [P, 2, D]), st.ps("turned", [P, 2, D])
        w_in, x_stored, t_stored = ([st.sem(f"{n}{s}") for s in range(2)] for n in ("w_in", "x_stored", "t_stored"))
        u_in, x_in = ([st.pool_sem(f"{n}{s}") for s in range(2)] for n in ("u_in", "x_in"))
        rows_in = st.pool_sem("rows_in")
        ident_ok, step, act_step, w_split = (st.sem(n) for n in ("ident_ok", "step", "act_step", "w_split"))
        sp_passed = st.sem("sp_passed")
        ev = lambda n, per=1, credit=0: Event(st, n, per, credit)
        u_split, y_ok, r_ok, out_ok = ev("u_split"), ev("y_ok", credit=2), ev("r_ok"), ev("out_ok", credit=2)
        r2_ok, xn_ok, turned_ok, xT_ok = ev("r2_ok"), ev("xn_ok"), ev("turned_ok", credit=2), ev("xT_ok", credit=2)
        block = st.block()

        def loop(eng, first, body):
            with eng.Fori(0, NT // 2 - 1) as i:
                for s in range(2):
                    body(i * 2 + s, i, s, False)
            for c in range(NT - 2, NT):
                body(c, c // 2, c % 2, True)

        @block.gpsimd
        def _(pool):
            make_identity(pool, ident[:, :], ident_ok)
            nc.gpsimd.memset(eps[:, :], EPS).then_inc(ident_ok, 1)
            pool.dma_start(gate[:, :], s_mod[:, gate_at:gate_at + D].to_broadcast([P, D])).then_inc(rows_in, 16)
            pool.dma_start(post[:, :], post_g.to_broadcast([P, D])).then_inc(rows_in, 16)

            def load(c, s):
                pool.dma_start(u[:, s], s_uT.rearrange("(k p) t -> p k t", p=P)[:, :, bass.ds(c * P, P)]).then_inc(u_in[s], 16)
                pool.dma_start(xt[:, s], x[bass.ds(c * P, P), :]).then_inc(x_in[s], 16)

            for s in range(2):
                load(s, s)
            with pool.Fori(0, NT // 2 - 1) as i:
                for s in range(2):
                    out_ok.wait(pool, i * 2 + s, 0)
                    load(i * 2 + (s + 2), s)

        @block.sync
        def _(sp):
            for k in range(KC):
                if k >= 2:
                    sp.wait_ge(w_split, k - 1)
                sp.dma_start(wraw[:, k % 2], w_out[k * P:(k + 1) * P, :]).then_inc(w_in[k % 2], 16)
            for s in range(2):
                sp.sem_inc(x_stored[s], 16)
                sp.sem_inc(t_stored[s], 16)

            def store(c, i, s, last):
                out_ok.wait(sp, c, 0)
                sp.sem_inc(sp_passed, 1)
                sp.dma_start(x_out[bass.ds(c * P, P), :], xo[:, s]).then_inc(x_stored[s], 16)
                if s_xnT is not None:
                    xT_ok.wait(sp, c, 0)
                    sp.sem_inc(sp_passed, 1)
                    sp.dma_start(s_xnT.rearrange("(k p) t -> p k t", p=P)[:, :, bass.ds(c * P, P)],
                                 xT[:, s].rearrange("p (k t) -> p k t", k=KC)).then_inc(t_stored[s], 16)

            loop(sp, 0, store)
            for s in range(2):
                sp.wait_ge(x_stored[s], 16 * (NT // 2 + 1))
                if s_xnT is not None:
                    sp.wait_ge(t_stored[s], 16 * (NT // 2 + 1))

        def project(pe, c, s):
            u_split.wait(pe, c, 0)
            out_ok.wait(pe, c, 0, back=2)
            for k in range(KC):
                for w, x in ((u_high, w_high), (u_high, w_low), (u_low, w_high)):
                    for half in range(2):
                        at = slice(half * BLK, (half + 1) * BLK)
                        ins = nc.tensor.matmul(y[:, s, at], w[:, s, k], x[:, k, at], start=k == 0 and w is u_high and x is w_high,
                                               stop=k == KC - 1 and w is u_low)
            y_ok.done(ins)

        @block.tensor
        def _(pe):
            pe.wait_ge(w_split, KC)
            pe.wait_ge(ident_ok, 3)
            project(pe, 0, 0)

            def body(c, i, s, last):
                if not (last and s == 1):
                    project(pe, c + 1, 1 - s)
                if s_xnT is not None:
                    xn_ok.wait(pe, c, 0)
                    xT_ok.wait(pe, c, 0, back=2)
                    for k in range(KC):
                        ins = nc.tensor.transpose(turned[:, s, k * P:(k + 1) * P], xn[:, s, k * P:(k + 1) * P], ident[:, :])
                    turned_ok.done(ins)

            loop(pe, 0, body)

        @block.vector
        def _(dve):
            v = nc.vector
            steps = Steps(dve, step)
            for e in (y_ok, out_ok, turned_ok, xT_ok):
                e.give_credit(dve)

            def split(c, i, s):
                dve.wait_ge(u_in[s], i * 16 + 16)
                steps.did(v.tensor_copy(u_high[:, s], u[:, s]))
                steps.wait()
                u_split.done(v.tensor_tensor(u_low[:, s], u[:, s], u_high[:, s].bitcast(F32), ALU.subtract))

            split(0, 0, 0)
            split(1, 0, 1)
            for k in range(KC):
                dve.wait_ge(w_in[k % 2], 16 * (k // 2 + 1))
                steps.did(v.tensor_copy(w_high[:, k], wraw[:, k % 2]))
                steps.wait()
                v.tensor_tensor(w_low[:, k], wraw[:, k % 2], w_high[:, k].bitcast(F32), ALU.subtract).then_inc(w_split, 1)
            dve.wait_ge(rows_in, 32)
            steps.did(v.tensor_tensor(gate[:, :], gate[:, :], post[:, :], ALU.mult))
            steps.wait()
            PER = 3
            start = steps.n

            def body(c, i, s, last):
                steps.restart(c * PER + start)
                y_ok.wait(dve, c, 0)
                r_ok.wait(dve, c, 0)
                dve.wait_ge(x_stored[s], i * 16 + 16)
                steps.did(v.scalar_tensor_tensor(xo[:, s], y[:, s], ss[:, s], gate[:, :], ALU.mult, ALU.mult))
                dve.wait_ge(x_in[s], i * 16 + 16)
                steps.wait()
                out_ok.done(v.tensor_tensor(xo[:, s], xo[:, s], xt[:, s], ALU.add))
                if s_xnT is not None:
                    r2_ok.wait(dve, c, 0)
                    turned_ok.wait(dve, c, 0, back=2)
                    xn_ok.done(v.tensor_scalar(xn[:, s], xo[:, s], ss[:, 2 + s], None, ALU.mult))
                if not last:
                    y_ok.wait(dve, c, 0)
                    split(c + 2, i + 1, s)
                else:
                    dve.sem_inc(step, 1)
                    steps.n += 1
                if s_xnT is not None:
                    turned_ok.wait(dve, c, 0)
                    dve.wait_ge(t_stored[s], i * 16 + 16)
                    xT_ok.done(v.tensor_copy(xT[:, s], turned[:, s]))
                assert steps.n == 2

            PER = 2
            loop(dve, 0, body)

        @block.scalar
        def _(act):
            a = nc.scalar
            act.wait_ge(ident_ok, 3)
            act.preload_act_table_set("natural_log_exp_and_others")
            steps = Steps(act, act_step)
            per = 5 if s_xnT is not None else 2

            def root(src, col, event, c):
                steps.did(a.activation(junk[:, col // 2], src, ACT.Square, accum_out=ss[:, col]))
                steps.wait()
                steps.did(a.activation(ss[:, col], ss[:, col], ACT.Ln, bias=eps[:, :], scale=1.0 / D))
                steps.wait()
                event.done(a.activation(ss[:, col], ss[:, col], ACT.Exp, scale=-0.5))

            def body(c, i, s, last):
                per = 2 if s_xnT is None else 4
                steps.restart(c * per)
                y_ok.wait(act, c, 0)
                out_ok.wait(act, c, 0, back=2)
                root(y[:, s], s, r_ok, c)
                if s_xnT is not None:
                    out_ok.wait(act, c, 0)
                    turned_ok.wait(act, c, 0, back=2)
                    root(xo[:, s], 2 + s, r2_ok, c)

            loop(act, 0, body)


def plain_projection(nc, name, s_xnT, s_mod, gain, shift_at, scale_at, w, first_scale, s_split, second, s_second,
                     gates=None):
    TPI = 4
    ITERS = 2 * D // P // TPI
    TILES = ITERS * TPI
    HALF = TILES // 2
    by_token = second == "by token"
    with Stage(nc, name) as st:
        obuf = st.sb("obuf", [P, 2, SEQ])
        parts = st.sb("parts", [P, 2, SEQ], F32R)
        h = Modulated(st, s_xnT, s_mod, gain, shift_at, scale_at, obuf[:, 0].rearrange("p (s t) -> p s t", s=4))
        wraw = st.sb("wraw", [P, KC, TPI * P])
        w_high, w_low = st.sb("w_high", [P, 2, KC, P], F32R), st.sb("w_low", [P, 2, KC, P], F32R)
        wg = st.sb("wg", [P, KC, BH])
        bias, ones = st.sb("bias", [BH, 1]), st.sb("ones", [BH, 1])
        ident = st.sb("ident", [P, P])
        y, turned = st.ps("y", [P, NB, BLK]), st.ps("turned", [P, NB, BLK])
        w_in, g_in = st.pool_sem("w_in"), st.pool_sem("g_in")
        ident_ok, w_split = st.sem("ident_ok"), st.sem("w_split")
        bank_full, bank_free, turned_ok, copied = (st.sem(n) for n in ("bank_full", "bank_free", "turned_ok", "copied"))
        parts_ok, dve_step, act_step, abs_ok = (st.sem(n) for n in ("parts_ok", "dve_step", "act_step", "abs_ok"))
        stored = [st.sem(f"stored{s}") for s in range(2)]
        p_stored, gates_stored = st.sem("p_stored"), st.sem("gates_stored")
        block = st.block()

        def weights(i):
            return w[:, bass.ds(i * (TPI * P), TPI * P)].rearrange("(k p) f -> p k f", p=P)

        @block.gpsimd
        def _(pool):
            make_identity(pool, ident[:, :], ident_ok)
            pool.dma_start(wraw[:, :, :], weights(0)).then_inc(w_in, 16)
            if gates:
                pool.dma_start(wg[:, :, :], w[:, 2 * D:2 * D + BH].rearrange("(k p) f -> p k f", p=P)).then_inc(g_in, 16)
                pool.dma_start(bias[:, :], gates[0]).then_inc(g_in, 16)
            with pool.Fori(1, ITERS) as i:
                pool.wait_ge(w_split, i * TPI)
                pool.dma_start(wraw[:, :, :], weights(i)).then_inc(w_in, 16)

        @block.sync
        def _(sp):
            sp.sem_inc(p_stored, 64)
            for s in range(2):
                sp.sem_inc(stored[s], 16)
            h.load(sp)
            for T in range(HALF):
                sp.wait_ge(parts_ok, T + 3)
                for a in range(2):
                    for low in range(2):
                        at = (2 * T + a) * P + (1 - low) * DH
                        sp.dma_start(s_split[at:at + DH, :], parts[a * DH:(a + 1) * DH, low].bitcast(F32)).then_inc(p_stored, 16)
            for i in range(TILES - HALF):
                if by_token:
                    sp.wait_ge(copied, i + 1)
                    sp.dma_start(s_second[:, i * P:(i + 1) * P].rearrange("(n t) f -> t n f", t=P),
                                 parts[:, i % 2].bitcast(F32).rearrange("t (n f) -> t n f", f=P)).then_inc(stored[i % 2], 16)
                else:
                    sp.wait_ge(bank_free, (HALF + i + 2) * NB)
                    sp.dma_start(s_second[i * P:(i + 1) * P, :], obuf[:, i % 2]).then_inc(stored[i % 2], 16)
            sp.wait_ge(p_stored, 64 * (HALF + 1))
            for s in range(2):
                sp.wait_ge(stored[s], 16 * (HALF // 2 + 1))
            if gates:
                sp.wait_ge(parts_ok, HALF + 3)
                for b in range(2):
                    sp.dma_start(gates[1][:, b, :], parts[0:BH, b].bitcast(F32)).then_inc(gates_stored, 16)
                sp.wait_ge(gates_stored, 32)

        def tensor_tile(pe, T, slot):
            pe.wait_ge(w_split, T + 1)
            for n in range(NB):
                pe.wait_ge(h.made, (n + 1) * KC)
                pe.wait_ge(bank_free, T * NB + (n + 1))
                three_passes(nc, y[:, n], w_high[:, slot], w_low[:, slot], h.high[:, :, n * BLK:(n + 1) * BLK],
                             h.low[:, :, n * BLK:(n + 1) * BLK]).then_inc(bank_full, 1)

        def turn(pe, T):
            pe.wait_ge(bank_free, (T + 2) * NB)
            if T > HALF:
                pe.wait_ge(copied, T - HALF)
            for n in range(NT):
                ins = nc.tensor.transpose(turned[:, n // 4, (n % 4) * P:(n % 4 + 1) * P],
                                          obuf[:, T % 2, n * P:(n + 1) * P], ident[:, :])
            ins.then_inc(turned_ok, 1)

        @block.tensor
        def _(pe):
            pe.wait_ge(ident_ok, 2)
            with pe.Fori(0, HALF // 2) as i:
                for t in range(2):
                    tensor_tile(pe, i * 2 + t, t)
            for T in range(HALF, TILES + (1 if gates else 0)):
                tensor_tile(pe, T, T % 2)
                if by_token and T > HALF:
                    turn(pe, T - 1)

        def split(dve, slot, raw, steps):
            steps.did(nc.vector.tensor_copy(w_high[:, slot, :, 0:raw.shape[2]], raw))
            steps.wait()
            nc.vector.tensor_tensor(w_low[:, slot, :, 0:raw.shape[2]], raw,
                                    w_high[:, slot, :, 0:raw.shape[2]].bitcast(F32), ALU.subtract).then_inc(w_split, 1)

        def split_next(dve, i, T, t, steps):
            dve.wait_ge(bank_full, T * NB + NB)
            dve.wait_ge(w_in, i * 16 + (32 if t >= 2 else 16))
            at = (t + 2) % TPI * P
            split(dve, t % 2, wraw[:, :, at:at + P], steps)

        def copy_turned(dve, T):
            i = T - HALF
            dve.wait_ge(turned_ok, i + 1)
            dve.wait_ge(stored[i % 2], 16 * (i // 2) + 16)
            dve.wait_ge(p_stored, 64 * (HALF + 1))
            nc.vector.tensor_copy(parts[:, i % 2].bitcast(F32), turned[:, :].rearrange("p a b -> p (a b)")).then_inc(copied, 1)

        @block.vector
        def _(dve):
            v = nc.vector
            dve.sem_inc(bank_free, NB)
            dve.sem_inc(parts_ok, 2)
            steps = Steps(dve, dve_step)
            dve.wait_ge(w_in, 16)
            for T in range(2):
                split(dve, T, wraw[:, :, T * P:(T + 1) * P], steps)
            h.make(dve)
            start = steps.n
            PER_ITER = TPI * 2
            with dve.Fori(0, ITERS // 2) as i:
                steps.restart(i * PER_ITER + start)
                for t in range(TPI):
                    T = i * TPI + t
                    split_next(dve, i, T, t, steps)
                    dve.wait_ge(bank_free, T * NB + 2 * NB)
                    dve.wait_ge(p_stored, T * 64 + 64)
                    steps.did(v.tensor_copy(parts[:, 0], obuf[:, t % 2]))
                    steps.wait()
                    v.tensor_tensor(parts[:, 1], obuf[:, t % 2], parts[:, 0].bitcast(F32), ALU.subtract).then_inc(parts_ok, 1)
                assert steps.n == PER_ITER
            steps.restart(ITERS // 2 * PER_ITER + start)
            for T in range(HALF, TILES):
                if T < TILES - 2:
                    split_next(dve, T // TPI, T, T % TPI, steps)
                elif gates and T == TILES - 2:
                    dve.wait_ge(bank_full, T * NB + NB)
                    dve.wait_ge(g_in, 32)
                    steps.did(v.memset(w_high[:, 0].bitcast(F32), 0.0))
                    steps.did(v.memset(w_low[:, 0].bitcast(F32), 0.0))
                    steps.wait()
                    split(dve, 0, wg[:, :, :], steps)
                if by_token and T > HALF:
                    copy_turned(dve, T - 1)
            if by_token:
                copy_turned(dve, TILES - 1)
            if gates:
                x, e = obuf[0:BH, 0], obuf[0:BH, 1]
                dve.wait_ge(bank_free, (TILES + 2) * NB)
                steps.did(v.memset(ones[:, :], 1.0))
                dve.wait_ge(turned_ok, HALF)
                v.scalar_tensor_tensor(e, x, -1.0, x, ALU.mult, ALU.max).then_inc(abs_ok, 1)
                dve.wait_ge(act_step, 2)
                steps.did(v.tensor_scalar(x, x, 0.0, None, ALU.min))
                steps.wait()
                steps.did(v.tensor_tensor(e, e, x, ALU.subtract))
                steps.wait()
                steps.did(v.tensor_tensor_scan(x, ones[:, 0:1].to_broadcast([BH, SEQ]), e, 0.0, ALU.mult, ALU.add))
                for s in range(2):
                    dve.wait_ge(stored[s], 16 * (HALF // 2 + 1))
                steps.wait()
                steps.did(v.tensor_copy(parts[0:BH, 0], x))
                steps.wait()
                v.tensor_tensor(parts[0:BH, 1], x, parts[0:BH, 0].bitcast(F32), ALU.subtract).then_inc(parts_ok, 1)

        @block.scalar
        def _(act):
            a = nc.scalar

            def evacuate(T, slot, func, scale, rows=P, **more):
                for n in range(NB):
                    act.wait_ge(bank_full, T * NB + (n + 1))
                    a.activation(obuf[0:rows, slot, n * BLK:(n + 1) * BLK], y[0:rows, n], func, scale=scale, **more)\
                     .then_inc(bank_free, 1)

            act.wait_ge(h.made, NB * KC)
            with act.Fori(0, HALF // 2) as i:
                for t in range(2):
                    act.wait_ge(parts_ok, i * 2 + (t + 1))
                    evacuate(i * 2 + t, t, ACT.Copy, first_scale)
            for T in range(HALF, TILES):
                i = T - HALF
                act.wait_ge(parts_ok, min(T, HALF + 1) + 1)
                if by_token and i >= 2:
                    act.wait_ge(turned_ok, i - 1)
                if not by_token:
                    act.wait_ge(stored[T % 2], 16 * (i // 2) + 16)
                evacuate(T, T % 2, ACT.Copy if by_token else ACT.Silu, 1.0)
            if gates:
                act.wait_ge(turned_ok, HALF - 1)
                act.wait_ge(g_in, 32)
                evacuate(TILES, 0, ACT.Identity, 1.0, BH, bias=bias[:, :])
                act.preload_act_table_set("natural_log_exp_and_others")
                act.wait_ge(abs_ok, 1)
                e = obuf[0:BH, 1]
                a.activation(e, e, ACT.Exp, scale=-1.0).then_inc(act_step, 1)
                act.wait_ge(act_step, 1)
                a.activation(e, e, ACT.Ln, bias=1.0).then_inc(act_step, 1)


def attention(nc, s_K, s_Fp, s_V, s_Q, s_ZT, s_u2T):
    PAIRS = BH // 2
    NQ = BLK // P
    MAIN = [(qb, kb) for qb in reversed(range(NB)) for kb in range(NQ * (qb + 1))]
    MAXI = [(qb, h, sub, grp) for qb in range(NB) for h in range(2) for sub in range(NQ) for grp in range(qb + 1)]
    STEPS, MAXS = len(MAIN), len(MAXI)
    ENDS = [j for j in range(STEPS) if j == STEPS - 1 or MAIN[j][0] != MAIN[j + 1][0]]
    ON_POOL = [(j, h) for j in range(STEPS) for h in range(2) if MAIN[j][0] and MAIN[j][1] % 2]
    ON_DVE = [(j, h) for j in range(STEPS) for h in range(2) if (j, h) not in ON_POOL]
    MAX_END = STEPS - 6
    with Stage(nc, "at") as st:
        K1, Q1, K2, Q2 = ([st.sb(f"{n}{s}", [P, 2, SEQ], F32R) for s in range(2)] for n in ("K1", "Q1", "K2", "Q2"))
        V = [st.sb(f"V{s}", [P, NT, P]) for s in range(2)]
        Z = [st.sb(f"Z{s}", [P, SEQ]) for s in range(2)]
        ident, ident_b, ones = st.sb("ident", [P, P]), st.sb("ident_b", [P, P], BF16), st.sb("ones", [P, DH])
        mask_q, mask_k = st.sb("mask_q", [P, P], BF16), st.sb("mask_k", [P, P], BF16)
        probs = st.sb("probs", [P, 3, 2, BLK])
        sum_v, sum_g = st.sb("sum_v", [P, 2, 2, BLK]), st.sb("sum_g", [P, 2, BLK])
        partial = st.sb("partial", [P, 2, NT, NB])
        top = st.sb("top", [P, 2 * NT])
        minus_top = st.sb("minus_top", [2 * NT, P], F32R)
        inv, u = st.sb("inv", [P, BLK]), st.sb("u", [P, 2, BLK])
        logits, rough = st.ps("logits", [P, 2, BLK]), st.ps("rough", [P, 2, BLK])
        o = st.ps("o", [P, 2, BLK])
        total, top_turned = st.ps("total", [P, BLK]), st.ps("top_turned", [P, BLK])
        one_in, two_in = ([[st.sem(f"{n}{s}{b}") for b in range(NB)] for s in range(2)] for n in ("one_in", "two_in"))
        u_stored = [st.sem(f"u_stored{s}") for s in range(2)]
        top_in = st.pool_sem("top_in")
        consts, rows_set, sp_passed, pool_passed = (st.sem(n) for n in ("consts", "rows_set", "sp_passed", "pool_passed"))
        ev = lambda n, per, credit=0: Event(st, n, per, credit)
        logits_ok, probs_ok, pv_ok = ev("logits_ok", 2 * STEPS), ev("probs_ok", 2 * STEPS, 2), ev("pv_ok", STEPS, 3)
        v_summed, g_summed = ev("v_summed", len(ON_DVE), 6), ev("g_summed", len(ON_POOL))
        joined, total_ok = ev("joined", 2 * (NB - 1), 2), ev("total_ok", NB, 2)
        logged, inv_ok = ev("logged", NB), ev("inv_ok", NB)
        rough_ok, reduced = ev("rough_ok", MAXS), ev("reduced", MAXS, 2)
        top_ok, top_turned_ok, minus_ok = ev("top_ok", 1, 1), ev("top_turned_ok", 1), ev("minus_ok", 1, 1)
        gated, u_ok = ev("gated", NB, 2), ev("u_ok", NB, 1)
        block = st.block()
        ONE, TWO = 3 * 16, 5 * 16

        def over_pairs(eng, body):
            with eng.Fori(0, PAIRS // 2 - 1) as i:
                for s in range(2):
                    body(i * 2 + s, i, s, True)
            for p in range(PAIRS - 2, PAIRS):
                body(p, p // 2, p % 2, p < PAIRS - 1)

        def late(j, lag):
            return [m for m, end in enumerate(ENDS) if end + lag == j]

        def width_from(j):
            qb, kb = MAIN[j]
            return max(0, kb - qb * NQ) * P

        @block.gpsimd
        def _(pool):
            g = nc.gpsimd
            g.memset(ident[:, :], 0.0)
            g.memset(ident_b[:, :], 0.0)
            g.memset(mask_q[:, :], 0.0)
            g.memset(mask_k[:, :], 0.0)
            g.memset(ones[:, :], 1.0)
            g.memset(partial[:, :, :, :], -BIG).then_inc(consts, 1)
            pool.wait_ge(consts, 1)
            sel = lambda x, fill, op, step, mult: g.affine_select(
                out=x[:, :], in_=x[:, :], compare_op=op, fill=fill, base=0, pattern=[[step, P]], channel_multiplier=mult)
            sel(ident, 1.0, ALU.not_equal, -1, 1)
            sel(ident_b, 1.0, ALU.not_equal, -1, 1)
            sel(mask_q, -BIG, ALU.is_ge, -1, 1)
            sel(mask_k, -BIG, ALU.is_ge, 1, -1).then_inc(consts, 1)
            for e in (probs_ok, pv_ok, v_summed, joined, total_ok, reduced, top_ok, minus_ok, gated, u_ok):
                e.give_credit(pool)
            for s in range(2):
                pool.sem_inc(u_stored[s], 16)

            def place(p, s):
                minus_ok.wait(pool, p, 0)
                pool.sem_inc(pool_passed, 1)
                for h in range(2):
                    pool.dma_start(Q1[s][DH + 2:DH + 3, h].bitcast(F32), minus_top[h * NT:(h + 1) * NT].bitcast(F32))\
                        .then_inc(top_in, 16)

            def body(p, i, s, more):
                for j in range(STEPS):
                    qb, kb = MAIN[j]
                    m = NB - 1 - qb
                    for h in range(2):
                        if (j, h) in ON_POOL:
                            at = ON_POOL.index((j, h))
                            off = width_from(j)
                            probs_ok.wait(pool, p, 2 * j + h)
                            x = probs[:, j % 3, h, off:BLK]
                            if kb == 1:
                                joined.wait(pool, p, 2 * m + h - 2)
                                pool.sem_inc(pool_passed, 1)
                                ins = g.tensor_copy(sum_g[:, h], x)
                            else:
                                g_summed.wait(pool, p, at - 2)
                                ins = g.tensor_tensor(sum_g[:, h, off:BLK], sum_g[:, h, off:BLK], x, ALU.add)
                            g_summed.done(ins)
                    if more and j == MAX_END + 3:
                        place(p + 1, 1 - s)

            place(0, 0)
            over_pairs(pool, body)

        def load(sp, p, s, n):
            at = slice(n * BLK, (n + 1) * BLK)
            pair = bass.ds(p * (2 * P), 2 * P)
            keys, queries = (x[pair, at].rearrange("(h w d) t -> w d h t", h=2, w=2) for x in (s_K, s_Q))
            for to, of in ((K1[s][0:DH, :, at], keys[1]), (Q1[s][0:DH, :, at], queries[1]),
                           (K1[s][DH:DH + 2, :, at], s_Fp[bass.ds(p * 2, 2), :, at].rearrange("h w t -> w h t"))):
                sp.dma_start(to.bitcast(F32), of).then_inc(one_in[s][n], 16)
            for to, of in ((K2[s][:, :, at].bitcast(F32), s_K[pair, at].rearrange("(h p) t -> p h t", p=P)),
                           (Q2[s][0:DH, :, at].bitcast(F32), queries[1]), (Q2[s][DH:P, :, at].bitcast(F32), queries[0]),
                           (V[s][:, n * NQ:(n + 1) * NQ], s_V[at, bass.ds(p * P, P)].rearrange("(k t) d -> t k d", t=P)),
                           (Z[s][:, at], s_ZT[bass.ds(p * P, P), at])):
                sp.dma_start(to, of).then_inc(two_in[s][n], 16)

        @block.sync
        def _(sp):
            sp.wait_ge(rows_set, 4)
            for s in range(2):
                for n in range(NB):
                    load(sp, s, s, n)

            def store(p, s, load_next):
                for m, n in enumerate(reversed(range(NB))):
                    u_ok.wait(sp, p, m)
                    sp.sem_inc(sp_passed, 1)
                    sp.dma_start(s_u2T[bass.ds(p * P, P), n * BLK:(n + 1) * BLK], u[:, m % 2]).then_inc(u_stored[m % 2], 16)
                    if load_next:
                        load(sp, p + 2, s, n)

            with sp.Fori(0, PAIRS // 2 - 1) as i:
                for s in range(2):
                    store(i * 2 + s, s, True)
            for p in range(PAIRS - 2, PAIRS):
                store(p, p % 2, False)
            for s in range(2):
                sp.wait_ge(u_stored[s], 16 * (PAIRS * NB // 2 + 1))

        def max_steps(j):
            return range(j * MAXS // MAX_END, (j + 1) * MAXS // MAX_END) if j < MAX_END else ()

        def rough_logits(pe, p, i, s, j):
            qb, h, sub, grp = MAXI[j]
            if j == 0 or qb != MAXI[j - 1][0]:
                pe.wait_ge(one_in[s][qb], i * ONE + ONE)
            width = BLK if grp < qb else (sub + 1) * P
            q_at = slice(qb * BLK + sub * P, qb * BLK + (sub + 1) * P)
            reduced.wait(pe, p, j - 2)
            ins = nc.tensor.matmul(rough[:, j % 2, 0:width], Q1[s][0:DH + 2, h, q_at],
                                   K1[s][0:DH + 2, h, grp * BLK:grp * BLK + width], start=True, stop=grp < qb)
            if grp == qb:
                ins = nc.tensor.matmul(rough[:, j % 2, sub * P:width], ident_b[:, :], mask_q[:, :], start=False, stop=True)
            rough_ok.done(ins)

        def reduce(dve, p, j):
            qb, h, sub, grp = MAXI[j]
            width = BLK if grp < qb else (sub + 1) * P
            if j == 0:
                top_ok.wait(dve, p, -1)
            rough_ok.wait(dve, p, j)
            reduced.done(nc.vector.tensor_reduce(partial[:, h, qb * NQ + sub, grp:grp + 1], rough[:, j % 2, 0:width],
                                                 AX.X, ALU.max))
            if j == MAXS - 1:
                reduced.wait(dve, p, j)
                minus_ok.wait(dve, p, -1)
                top_ok.done(nc.vector.tensor_reduce(top[:, :], partial[:, :, :, :].rearrange("p h t g -> p (h t) g"),
                                                    AX.X, ALU.max))

        def turn_top(pe, p):
            top_ok.wait(pe, p, 0)
            minus_ok.wait(pe, p, -1)
            top_turned_ok.done(nc.tensor.transpose(top_turned[0:2 * NT, 0:P], top[:, :], ident[:, :]))

        def negate_top(act, p):
            top_turned_ok.wait(act, p, 0)
            minus_ok.done(nc.scalar.activation(minus_top[:, :], top_turned[0:2 * NT, 0:P], ACT.Copy, scale=-1.0))

        def exact_logits(pe, p, j, h, s):
            qb, kb = MAIN[j]
            off = width_from(j)
            q_at, k_at = slice(qb * BLK + off, (qb + 1) * BLK), slice(kb * P, (kb + 1) * P)
            probs_ok.wait(pe, p, 2 * j + h - 2)
            out = logits[:, h, off:BLK]
            nc.tensor.matmul(out, K1[s][0:DH + 3, h, k_at], Q1[s][0:DH + 3, h, q_at], start=True, stop=False)
            if kb >= qb * NQ:
                nc.tensor.matmul(logits[:, h, off:off + P], ident_b[:, :], mask_k[:, :], start=False, stop=False)
            logits_ok.done(nc.tensor.matmul(out, K2[s][:, h, k_at], Q2[s][:, h, q_at], start=False, stop=True))

        def sum_values(pe, p, j, s):
            qb, kb = MAIN[j]
            m = NB - 1 - qb
            off = width_from(j)
            if kb == 0:
                gated.wait(pe, p, m - 2)
            probs_ok.wait(pe, p, 2 * j + 1)
            for h in range(2):
                at = slice(h * DH, (h + 1) * DH)
                ins = nc.tensor.matmul(o[at, m % 2, off:BLK], V[s][:, kb, at], probs[:, j % 3, h, off:BLK],
                                       start=kb == 0, stop=kb == NQ * (qb + 1) - 1)
            pv_ok.done(ins)

        def sum_tiles(pe, p, m):
            if m < NB - 1:
                joined.wait(pe, p, 2 * m + 1)
            else:
                v_summed.wait(pe, p, len(ON_DVE) - 1)
            if m:
                inv_ok.wait(pe, p, m - 1)
            for h in range(2):
                ins = nc.tensor.matmul(total[h * DH:(h + 1) * DH], ones[:, :], sum_v[:, m % 2, h], start=True, stop=True)
            total_ok.done(ins)

        @block.tensor
        def _(pe):
            pe.wait_ge(consts, 2)
            for j in range(MAXS):
                rough_logits(pe, 0, 0, 0, j)
            turn_top(pe, 0)

            def body(p, i, s, more):
                for n in range(NB):
                    pe.wait_ge(two_in[s][n], i * TWO + TWO)
                pe.wait_ge(top_in, p * 32 + 32)
                for j in range(STEPS + 3):
                    if j < STEPS:
                        exact_logits(pe, p, j, 0, s)
                        exact_logits(pe, p, j, 1, s)
                        if more:
                            for r in max_steps(j):
                                rough_logits(pe, p + 1, i + s, 1 - s, r)
                    if 1 <= j <= STEPS:
                        sum_values(pe, p, j - 1, s)
                    for m in late(j, 3):
                        sum_tiles(pe, p, m)
                    if more and j == MAX_END + 1:
                        turn_top(pe, p + 1)

            over_pairs(pe, body)

        @block.vector
        def _(dve):
            v = nc.vector
            for s in range(2):
                for x in (K1, Q1):
                    v.memset(x[s][DH:DH + 3].bitcast(F32), 1.0).then_inc(rows_set, 1)
            dve.wait_ge(consts, 2)
            for j in range(MAXS):
                reduce(dve, 0, j)

            def add_up(p, j, h):
                qb, kb = MAIN[j]
                m, off, at = NB - 1 - qb, width_from(j), ON_DVE.index((j, h))
                probs_ok.wait(dve, p, 2 * j + h)
                x, to = probs[:, j % 3, h, off:BLK], sum_v[:, m % 2, h, off:BLK]
                if kb == 0:
                    total_ok.wait(dve, p, m - 2)
                    ins = v.tensor_copy(to, x)
                else:
                    v_summed.wait(dve, p, at - 2)
                    ins = v.tensor_tensor(to, to, x, ALU.add)
                v_summed.done(ins)

            def join(p, m):
                for h in range(2):
                    g_summed.wait(dve, p, max(n for n, (j, hh) in enumerate(ON_POOL) if hh == h and MAIN[j][0] == NB - 1 - m))
                    v_summed.wait(dve, p, max(n for n, (j, hh) in enumerate(ON_DVE) if hh == h and MAIN[j][0] == NB - 1 - m))
                    joined.done(v.tensor_tensor(sum_v[:, m % 2, h], sum_v[:, m % 2, h], sum_g[:, h], ALU.add))

            def gate(p, i, s, m):
                n = NB - 1 - m
                pv_ok.wait(dve, p, ENDS[m])
                dve.wait_ge(two_in[s][n], i * TWO + TWO)
                dve.wait_ge(u_stored[m % 2], p * (16 * NB // 2) + 16 * (m // 2 + 1))
                gated.done(v.tensor_tensor(u[:, m % 2], o[:, m % 2], Z[s][:, n * BLK:(n + 1) * BLK], ALU.mult))

            def normalize(p, m):
                inv_ok.wait(dve, p, m)
                gated.wait(dve, p, m)
                u_ok.done(v.tensor_tensor(u[:, m % 2], u[:, m % 2], inv[:, :], ALU.mult))

            def body(p, i, s, more):
                for j in range(STEPS + 5):
                    if more and j < STEPS:
                        for r in max_steps(j):
                            reduce(dve, p + 1, r)
                    if j < STEPS:
                        for h in range(2):
                            if (j, h) in ON_DVE:
                                add_up(p, j, h)
                    for m in late(j, 1):
                        if m < NB - 1:
                            join(p, m)
                    for m in late(j, 2):
                        gate(p, i, s, m)
                    for m in late(j, 4):
                        normalize(p, m)

            over_pairs(dve, body)

        @block.scalar
        def _(act):
            act.preload_act_table_set("natural_log_exp_and_others")
            negate_top(act, 0)

            def summed(p, j, h):
                if (j % STEPS, h) in ON_POOL:
                    g_summed.wait(act, p, ON_POOL.index((j, h)))
                else:
                    v_summed.wait(act, p, ON_DVE.index((j % STEPS, h)) - (len(ON_DVE) if j < 0 else 0))

            def body(p, i, s, more):
                for j in range(STEPS + 4):
                    if j < STEPS:
                        off = width_from(j)
                        for h in range(2):
                            logits_ok.wait(act, p, 2 * j + h)
                            pv_ok.wait(act, p, j - 3)
                            summed(p, j - 3, h)
                            probs_ok.done(nc.scalar.activation(probs[:, j % 3, h, off:BLK], logits[:, h, off:BLK], ACT.Exp))
                    for m in late(j, 3):
                        total_ok.wait(act, p, m)
                        u_ok.wait(act, p, m - 1)
                        logged.done(nc.scalar.activation(inv[:, :], total[:, :], ACT.Ln))
                        logged.wait(act, p, m)
                        inv_ok.done(nc.scalar.activation(inv[:, :], inv[:, :], ACT.Exp, scale=-1.0))
                    if more and j == MAX_END + 1:
                        act.wait_ge(top_in, p * 32 + 32)
                        negate_top(act, p + 1)

            over_pairs(act, body)


_INS = ["x", "c", "a_mod_w", "a_mod_b", "a_pre_g", "a_post_g", "a_w_in", "a_conv_w", "a_a_log", "a_dt_bias",
        "a_o_gain", "a_w_out", "kv_mod_w", "kv_mod_b", "kv_norm_g", "kv_w", "kv_b_f",
        "b_mod_w", "b_mod_b", "b_pre_g", "b_post_g", "b_w_in", "b_w_out"]


def build(nc, a, out):
    dram = lambda name, shape, dt=F32: nc.dram_tensor(name, shape, dt).ap()
    s_mod = dram("s_mod", (1, 8 * D))
    s_xnT = dram("s_xnT0", (D, SEQ))
    s_qkv = dram("s_qkv", (3 * D + P, SEQ))
    s_zT = dram("s_zT", (D, SEQ))
    s_abT = dram("s_abT", (2 * AH, SEQ))
    modulation(nc, a["c_cols"], [(a["a_mod_w"][0], a["a_mod_b"][0]), (a["kv_mod_w"], a["kv_mod_b"]),
                            (a["b_mod_w"][0], a["b_mod_b"][0])], s_mod)
    normalize_input(nc, a["x"], s_xnT)
    deltanet_projection(nc, s_xnT, s_mod, a["a_pre_cols"], a["a_w_in"][0], a["taps"], s_qkv, s_zT, s_abT)
    s_g, s_uT = dram("s_g", (AH, SEQ)), dram("s_uT", (D, SEQ))
    delta_rule(nc, s_qkv, s_zT, s_abT, a["a_log_col"], a["dt_bias_col"], a["o_gain_col"], a["level_masks"], s_g, s_uT)
    s_x1, s_xnT1 = dram("s_x1", (SEQ, D)), dram("s_xnT", (D, SEQ))
    output_projection(nc, "oa", s_uT, a["a_w_out"][0], s_mod, 2 * D, a["a_post_g"], a["x"][0], s_x1, s_xnT1)
    s_K, s_V, s_F = dram("s_K", (BH * P, SEQ)), dram("s_V", (SEQ, D)), dram("s_Fp", (BH, 2, SEQ))
    plain_projection(nc, "pk", s_xnT1, s_mod, a["kv_norm_cols"], 3 * D, 4 * D, a["kv_w"], 1.0, s_K, "by token", s_V,
                     (a["kv_b_f_col"], s_F))
    s_Q, s_ZT = dram("s_Q", (BH * P, SEQ)), dram("s_ZT", (D, SEQ))
    plain_projection(nc, "pb", s_xnT1, s_mod, a["b_pre_cols"], 5 * D, 6 * D, a["b_w_in"][0], DH ** -0.5, s_Q, "silu", s_ZT)
    s_u2T = dram("s_u2T", (D, SEQ))
    nc.disable_value_cache = True
    attention(nc, s_K, s_F, s_V, s_Q, s_ZT, s_u2T)
    nc.disable_value_cache = False
    output_projection(nc, "ob", s_u2T, a["b_w_out"][0], s_mod, 7 * D, a["b_post_g"], s_x1, out[0], None)


def kernel(**inputs):
    import numpy as np
    import concourse.bacc as bacc
    from concourse.bass_utils import run_bass_kernel_spmd

    nc = bacc.Bacc("TRN2", target_bir_lowering=False, num_devices=1)
    arrays, aps = {}, {}

    def give(name, array):
        array = np.ascontiguousarray(array)
        arrays[f"in_{name}_dram"] = array
        aps[name] = nc.dram_tensor(f"in_{name}_dram", array.shape, mybir.dt.from_np(array.dtype), kind="ExternalInput").ap()

    for name in _INS:
        give(name, inputs[name])
    give("taps", np.asarray(inputs["a_conv_w"])[0].reshape(4, 3 * AH, P).transpose(2, 1, 0))
    for name, of in (("c_cols", "c"), ("a_pre_cols", "a_pre_g"), ("kv_norm_cols", "kv_norm_g"), ("b_pre_cols", "b_pre_g")):
        give(name, np.asarray(inputs[of]).reshape(KC, P).T)
    for name, of in (("a_log_col", "a_a_log"), ("dt_bias_col", "a_dt_bias"), ("o_gain_col", "a_o_gain"), ("kv_b_f_col", "kv_b_f")):
        give(name, np.asarray(inputs[of]).reshape(-1, 1))
    row, col = np.arange(P)[:, None], np.arange(P)[None, :]
    below = np.stack([((row >> l) == (col >> l) + 1) & ((row >> l) % 2 == 1) for l in range(7)], axis=1)
    give("level_masks", np.stack([below, below.transpose(2, 1, 0)], axis=1).astype(np.float32))
    out = nc.dram_tensor("out_0_dram", (1, SEQ, D), F32, kind="ExternalOutput").ap()
    build(nc, aps, out)
    result = run_bass_kernel_spmd(nc, [arrays], core_ids=[0])
    return result.results[0]["out_0_dram"]
```

```python
from contextlib import ExitStack

import concourse.bass as bass
from concourse import mybir

F32 = mybir.dt.float32
F32R = mybir.dt.float32r
BF16 = mybir.dt.bfloat16
U8 = mybir.dt.uint8
ALU = mybir.AluOpType
ACT = mybir.ActivationFunctionType
AX = mybir.AxisListType

P = 128
D = 1024
KC = D // P
SEQ = 2048
BLK = 512
NB = SEQ // BLK
NT = SEQ // P
AH = 8
BH = 16
DH = 64
EPS = 1e-6
BIG = 1.0e30


class Stage:

    def __init__(self, nc, name):
        self.nc, self.name, self.ctx, self.sems = nc, name, ExitStack(), []

    def __enter__(self):
        self.ctx.__enter__()
        return self

    def __exit__(self, *e):
        self.ctx.__exit__(*e)
        self.nc.clear_and_free_semaphores(self.sems)
        self.nc.all_engine_barrier()

    def sb(self, name, shape, dt=F32):
        return self.ctx.enter_context(self.nc.sbuf_tensor(f"{self.name}_{name}", shape, dt))

    def ps(self, name, shape, dt=F32):
        return self.ctx.enter_context(self.nc.psum_tensor(f"{self.name}_{name}", shape, dt))

    def sem(self, name):
        self.sems.append(self.nc.alloc_semaphore(f"{self.name}_{name}"))
        return self.sems[-1]

    def pool_sem(self, name):
        return self.nc.alloc_semaphore(f"{self.name}_{name}")

    def block(self):
        return self.ctx.enter_context(self.nc.Block())


class Steps:

    def __init__(self, eng, sem):
        self.eng, self.sem, self.base, self.n = eng, sem, 0, 0

    def restart(self, base):
        self.base, self.n = base, 0

    def did(self, ins):
        ins.then_inc(self.sem, 1)
        self.n += 1

    def wait(self):
        self.eng.wait_ge(self.sem, self.base + self.n)


def make_identity(pool, ident, sem):
    pool.memset(ident, 0.0).then_inc(sem, 1)
    pool.wait_ge(sem, 1)
    pool.affine_select(out=ident, in_=ident, compare_op=ALU.not_equal, fill=1.0, base=0,
                       pattern=[[-1, P]], channel_multiplier=1).then_inc(sem, 1)


def begin(nc, c, weights, s_mod, x, s_xnT):
    pieces = [(w, b, j) for w, b in weights for j in range(w.shape[1] // D)]
    assert NT == 2 * len(pieces)
    QW, QS = D // 4, P // 4
    with Stage(nc, "st") as st:
        ccol, csil = st.sb("ccol", [P, KC]), st.sb("csil", [P, KC])
        w_sb = st.sb("w", [P, 3, KC, D])
        bias, row = st.sb("bias", [P, 2, QW]), st.sb("row", [P, 2, QW])
        acc = st.ps("acc", [P, 2, BLK])
        c_in, c_ready, summed, added = (st.sem(n) for n in ("c_in", "c_ready", "summed", "added"))
        w_in = [st.sem(f"w_in{s}") for s in range(3)]
        b_in, row_stored = ([st.pool_sem(f"{n}{s}") for s in range(2)] for n in ("b_in", "row_stored"))
        ident, eps = st.sb("ident", [P, P]), st.sb("eps", [P, 1])
        xt = st.sb("x", [P, 4, D])
        xn, outT = st.sb("xn", [P, 2, D]), st.sb("outT", [P, 2, D])
        junk = st.sb("junk", [P, D])
        ss, rstd = st.sb("ss", [P, NT]), st.sb("rstd", [P, NT])
        turned = st.ps("turned", [P, 2, 2, BLK])
        x_in = [st.sem(f"x_in{s}") for s in range(4)]
        ident_ok, eps_ok, squared, logged, rooted = (st.sem(n) for n in ("ident_ok", "eps_ok", "squared", "logged", "rooted"))
        scaled, turned_ok, copied = (st.sem(n) for n in ("scaled", "turned_ok", "copied"))
        stored = [st.pool_sem(f"stored{s}") for s in range(2)]
        block = st.block()

        @block.sync
        def _(sp):
            sp.dma_start(ccol[:, :], c).then_inc(c_in, 16)

            def load_x(i):
                if i >= 4:
                    sp.wait_ge(scaled, i - 3)
                sp.dma_start(xt[:, i % 4], x[0, i * P:(i + 1) * P, :]).then_inc(x_in[i % 4], 16)

            load_x(0)
            load_x(1)
            for n, (w, b, j) in enumerate(pieces):
                if n >= 3:
                    sp.wait_ge(summed, 2 * (n - 2))
                sp.dma_start(w_sb[:, n % 3], w[:, j * D:(j + 1) * D].rearrange("(k p) f -> p k f", p=P))\
                  .then_inc(w_in[n % 3], 16)
                for i in (2 * n + 2, 2 * n + 3):
                    if i < NT:
                        load_x(i)

        @block.gpsimd
        def _(pool):
            pool.memset(eps[:, :], EPS).then_inc(eps_ok, 1)
            make_identity(pool, ident[:, :], ident_ok)
            for i in range(NT + 2):
                n, first = i // 2, i % 2 == 0
                if first:
                    if n >= 1:
                        pool.wait_ge(added, 4 * n)
                        pool.dma_start(s_mod[0, (n - 1) * D:n * D].rearrange("(q f) -> q f", f=QW), row[0:P:QS, (n - 1) % 2])\
                            .then_inc(row_stored[(n - 1) % 2], 16)
                    if n < len(pieces):
                        b, j = pieces[n][1:]
                        pool.dma_start(bias[0:P:QS, n % 2], b[j * D:(j + 1) * D].rearrange("(q f) -> q f", f=QW))\
                            .then_inc(b_in[n % 2], 16)
                if i < NT:
                    pool.wait_ge(copied, i + 1)
                    pool.dma_start(s_xnT.rearrange("(k p) t -> p k t", p=P)[:, :, i * P:(i + 1) * P],
                                   outT[:, i % 2].rearrange("p (k t) -> p k t", k=KC)).then_inc(stored[i % 2], 16)
            for s in range(2):
                pool.wait_ge(row_stored[s], 16 * (len(pieces) // 2))
                pool.wait_ge(stored[s], 16 * (NT // 2))

        @block.scalar
        def _(act):
            act.wait_ge(c_in, 16)
            nc.scalar.activation(csil[:, :], ccol[:, :], ACT.Silu).then_inc(c_ready, 1)
            act.preload_act_table_set("natural_log_exp_and_others")
            act.wait_ge(eps_ok, 1)
            for i in range(NT):
                act.wait_ge(x_in[i % 4], 16 * (i // 4 + 1))
                if i:
                    act.wait_ge(squared, i)
                nc.scalar.activation(junk[:, :], xt[:, i % 4], ACT.Square, accum_out=ss[:, i:i + 1]).then_inc(squared, 1)
                act.wait_ge(squared, i + 1)
                nc.scalar.activation(ss[:, i:i + 1], ss[:, i:i + 1], ACT.Ln, bias=eps[:, :], scale=1.0 / D)\
                    .then_inc(logged, 1)
                act.wait_ge(logged, i + 1)
                nc.scalar.activation(rstd[:, i:i + 1], ss[:, i:i + 1], ACT.Exp, scale=-0.5).then_inc(rooted, 1)

        @block.vector
        def _(dve):
            for i in range(NT + 1):
                if i < NT:
                    dve.wait_ge(rooted, i + 1)
                    if i >= 2:
                        dve.wait_ge(turned_ok, i - 1)
                    nc.vector.tensor_scalar(xn[:, i % 2], xt[:, i % 4], rstd[:, i:i + 1], None, ALU.mult).then_inc(scaled, 1)
                if i >= 1:
                    j = i - 1
                    dve.wait_ge(turned_ok, j + 1)
                    if j >= 2:
                        dve.wait_ge(stored[j % 2], 16 * (j // 2))
                    nc.vector.tensor_copy(outT[:, j % 2], turned[:, j % 2].rearrange("p a b -> p (a b)")).then_inc(copied, 1)
                if i and i % 2 == 0:
                    n = i // 2 - 1
                    dve.wait_ge(summed, 2 * (n + 1))
                    dve.wait_ge(b_in[n % 2], 16 * (n // 2 + 1))
                    if n >= 2:
                        dve.wait_ge(row_stored[n % 2], 16 * (n // 2))
                    for at in range(0, P, QS):
                        nc.vector.tensor_tensor(row[at:at + 1, n % 2], acc[at:at + 1, n % 2, 0:QW], bias[at:at + 1, n % 2],
                                                ALU.add).then_inc(added, 1)

        @block.tensor
        def _(pe):
            pe.wait_ge(ident_ok, 2)
            pe.wait_ge(c_ready, 1)
            for i in range(NT):
                n, half = i // 2, i % 2
                pe.wait_ge(scaled, i + 1)
                if i >= 2:
                    pe.wait_ge(copied, i - 1)
                for k in range(KC):
                    ins = nc.tensor.transpose(turned[:, i % 2, k // 4, (k % 4) * P:(k % 4 + 1) * P],
                                              xn[:, i % 2, k * P:(k + 1) * P], ident[:, :])
                ins.then_inc(turned_ok, 1)
                if half == 0:
                    pe.wait_ge(w_in[n % 3], 16 * (n // 3 + 1))
                    if n >= 2:
                        pe.wait_ge(added, 4 * (n - 1))
                for k in range(half * KC // 2, (half + 1) * KC // 2):
                    for at in range(4):
                        ins = nc.tensor.matmul(acc[at * QS:at * QS + 1, n % 2, 0:QW], csil[:, k:k + 1],
                                               w_sb[:, n % 3, k, at * QW:(at + 1) * QW], start=k == 0, stop=k == KC - 1)
                ins.then_inc(summed, 1)


class Modulated:

    def __init__(self, st, s_xnT, s_mod, gain, shift_at, scale_at, scratch):
        self.st, self.nc = st, st.nc
        self.src, self.mod, self.gain, self.shift_at, self.scale_at = s_xnT, s_mod, gain, shift_at, scale_at
        self.high = st.sb("h_high", [P, KC, SEQ], F32R)
        self.low = st.sb("h_low", [P, KC, SEQ], F32R)
        self.cols = st.sb("mod_cols", [P, 3, KC])
        self.slots = scratch
        self.n_slots = len(scratch)
        self.cols_in = st.sem("cols_in")
        self.x_in = [st.sem(f"xb_in{s}") for s in range(self.n_slots)]
        self.made, self.cols_ok, self.scaled = (st.sem(n) for n in ("h_made", "h_cols_ok", "h_scaled"))
        self.rounded = [st.sem(f"h_rounded{n}") for n in ("_even", "_odd")]

    def load_columns(self, sp):
        sp.dma_start(self.cols[:, 0], self.gain).then_inc(self.cols_in, 16)
        for n, at in ((1, self.scale_at), (2, self.shift_at)):
            sp.dma_start(self.cols[:, n], self.mod[0, at:at + D].rearrange("(k p) -> p k", p=P),
                         allow_slow_non_contiguous=True).then_inc(self.cols_in, 16)

    def load(self, sp, parts):
        for m in parts:
            n, k = m // KC, m % KC
            if m >= self.n_slots:
                sp.wait_ge(self.made, m - self.n_slots + 1)
            sp.dma_start(self.slots[m % self.n_slots], self.src[k * P:(k + 1) * P, n * BLK:(n + 1) * BLK])\
              .then_inc(self.x_in[m % self.n_slots], 16)

    def block(self, m):
        n, k = m // KC, m % KC
        return [t[:, k, n * BLK:(n + 1) * BLK] for t in (self.high, self.low)]

    def scale(self, act):
        a = self.nc.scalar
        act.wait_ge(self.cols_ok, 2)
        for m in range(NB * KC):
            k, x, high = m % KC, self.slots[m % self.n_slots], self.block(m)[0]
            act.wait_ge(self.x_in[m % self.n_slots], 16 * (m // self.n_slots + 1))
            a.activation(x, x, ACT.Identity, scale=self.cols[:, 0, k:k + 1], bias=self.cols[:, 2, k:k + 1])\
             .then_inc(self.scaled, 1)
            if m % 2 == 0:
                act.wait_ge(self.scaled, m + 1)
                a.activation(high, x, ACT.Copy).then_inc(self.rounded[0], 1)

    def make_columns(self, dve):
        v = self.nc.vector
        dve.wait_ge(self.cols_in, 48)
        v.tensor_scalar(self.cols[:, 1], self.cols[:, 1], 1.0, None, ALU.add).then_inc(self.cols_ok, 1)
        dve.wait_ge(self.cols_ok, 1)
        v.tensor_tensor(self.cols[:, 0], self.cols[:, 0], self.cols[:, 1], ALU.mult).then_inc(self.cols_ok, 1)

    def make(self, dve, parts):
        v = self.nc.vector
        for m in parts:
            x, (high, low) = self.slots[m % self.n_slots], self.block(m)
            if m % 2:
                dve.wait_ge(self.scaled, m + 1)
                v.tensor_copy(high, x).then_inc(self.rounded[1], 1)
            dve.wait_ge(self.rounded[m % 2], m // 2 + 1)
            v.tensor_tensor(low, x, high.bitcast(F32), ALU.subtract).then_inc(self.made, 1)


def three_passes(nc, out, w_high, w_low, h_high, h_low):
    for k in range(KC):
        nc.tensor.matmul(out, w_high[:, k], h_high[:, k], start=k == 0, stop=False)
        nc.tensor.matmul(out, w_high[:, k], h_low[:, k], start=False, stop=False)
        ins = nc.tensor.matmul(out, w_low[:, k], h_high[:, k], start=False, stop=k == KC - 1)
    return ins


def deltanet_projection(nc, s_xnT, s_mod, a_pre_g, a_w_in, a_conv_w, s_qkv, s_zT, s_abT):
    TPI = 4
    PER = TPI * NB
    QK_ITERS, V_ITERS, Z_ITERS = 2 * AH // TPI, AH // TPI, AH // TPI
    ITERS = QK_ITERS + V_ITERS + Z_ITERS
    with Stage(nc, "pa") as st:
        ybuf = st.sb("ybuf", [P, 2, 3 + SEQ])
        acc = st.sb("acc", [P, SEQ])
        sil = st.sb("sil", [P, SEQ])
        sq = st.sb("sq", [P, SEQ])
        h = Modulated(st, s_xnT, s_mod, a_pre_g, 0, D, [x[:, n * BLK:(n + 1) * BLK] for x in (sq, sil) for n in range(NB)])
        wraw = st.sb("wraw", [P, KC, TPI * P])
        w_high = st.sb("w_high", [P, 2, KC, P], F32R)
        w_low = st.sb("w_low", [P, 2, KC, P], F32R)
        wab = st.sb("wab", [P, KC, 2 * AH])
        taps = st.sb("taps", [P, 3 * AH, 4])
        ones = st.sb("ones", [P, P])
        eps = st.sb("eps", [P, 1])
        y = st.ps("y", [P, NB, BLK])
        norm = st.ps("norm", [P, NB, BLK])
        taps_in, w_first, w_in, ab_in = (st.sem(n) for n in ("taps_in", "w_first", "w_in", "ab_in"))
        consts_set = st.sem("consts_set")
        w_split, bank_full, bank_free = st.sem("w_split"), st.sem("bank_full"), st.sem("bank_free")
        convolved, silu_done, squared = st.sem("convolved"), st.sem("silu_done"), st.sem("squared")
        summed, rooted, scaled, stored = st.sem("summed"), st.sem("rooted"), st.sem("scaled"), st.pool_sem("stored")
        dve_step, act_step = st.sem("dve_step"), st.sem("act_step")
        block = st.block()

        def weights(i):
            return a_w_in[:, bass.ds(i * (TPI * P), TPI * P)].rearrange("(k p) f -> p k f", p=P)

        @block.sync
        def _(sp):
            h.load_columns(sp)
            h.load(sp, range(KC))
            sp.dma_start(wraw[:, :, 0:2 * P], weights(0)[:, :, 0:2 * P]).then_inc(w_first, 16)
            h.load(sp, range(KC, 2 * KC))
            sp.dma_start(wraw[:, :, 2 * P:], weights(0)[:, :, 2 * P:]).then_inc(w_in, 16)
            h.load(sp, range(2 * KC, NB * KC))
            sp.dma_start(taps[:, :, :], a_conv_w).then_inc(taps_in, 16)
            sp.dma_start(wab[:, :, :], a_w_in[:, 4 * D:4 * D + 2 * AH].rearrange("(k p) f -> p k f", p=P))\
              .then_inc(ab_in, 16)
            with sp.Fori(1, ITERS) as i:
                sp.wait_ge(w_split, i * TPI)
                sp.dma_start(wraw[:, :, :], weights(i)).then_inc(w_in, 16)

        def tensor_tile(pe, T, slot, norm_before):
            pe.wait_ge(w_split, T + 1)
            for n in range(NB):
                pe.wait_ge(h.made, (n + 1) * KC)
                pe.wait_ge(bank_free, T * NB + (n + 1))
                three_passes(nc, y[:, n], w_high[:, slot], w_low[:, slot], h.high[:, :, n * BLK:(n + 1) * BLK],
                             h.low[:, :, n * BLK:(n + 1) * BLK]).then_inc(bank_full, 1)
            if norm_before:
                pe.wait_ge(squared, T + 1)
                for n in range(NB):
                    ins = nc.tensor.matmul(norm[:, n], ones[:, :], sq[:, n * BLK:(n + 1) * BLK], start=True, stop=True)
                ins.then_inc(summed, 1)

        @block.tensor
        def _(pe):
            pe.wait_ge(consts_set, 1)
            with pe.Fori(0, QK_ITERS) as i:
                for t in range(TPI):
                    tensor_tile(pe, i * TPI + t, t % 2, True)
            for T in range(QK_ITERS * TPI, ITERS * TPI + 1):
                tensor_tile(pe, T, T % 2, T == QK_ITERS * TPI)

        def split(dve, slot, raw, steps):
            steps.did(nc.vector.tensor_copy(w_high[:, slot, :, 0:raw.shape[2]], raw))
            steps.wait()
            nc.vector.tensor_tensor(w_low[:, slot, :, 0:raw.shape[2]], raw,
                                    w_high[:, slot, :, 0:raw.shape[2]].bitcast(F32), ALU.subtract).then_inc(w_split, 1)

        def vector_tile(dve, i, T, t, norm_before, convolve, steps):
            dve.wait_ge(bank_full, T * NB + NB)
            if t == 0:
                dve.wait_ge(w_in, (i + 1) * 16)
            if t == 2:
                dve.wait_ge(w_in, (i + 2) * 16)
            at = (t + 2) % TPI * P
            split(dve, t % 2, wraw[:, :, at:at + P], steps)
            post(dve, T, t % 2, norm_before, convolve, steps)

        def post(dve, T, slot, norm_before, convolve, steps):
            if norm_before:
                dve.wait_ge(rooted, T + 1)
                nc.vector.tensor_tensor(sil[:, :], sil[:, :], sq[:, :], ALU.mult).then_inc(scaled, 1)
            if convolve:
                dve.wait_ge(bank_free, T * NB + 2 * NB)
                dve.wait_ge(silu_done, T + 1)
                for j in range(4):
                    x = ybuf[:, slot, j:j + SEQ]
                    w = taps[:, bass.ds(T, 1), j:j + 1].rearrange("p a b -> p (a b)")
                    if j == 0:
                        steps.did(nc.vector.tensor_scalar(acc[:, :], x, w, None, ALU.mult))
                        continue
                    steps.wait()
                    ins = nc.vector.scalar_tensor_tensor(acc[:, :], x, w, acc[:, :], ALU.mult, ALU.add)
                    steps.did(ins) if j < 3 else ins.then_inc(convolved, 1)

        @block.vector
        def _(dve):
            nc.vector.memset(ones[:, :], 1.0).then_inc(consts_set, 1)
            nc.vector.memset(eps[:, :], EPS)
            nc.vector.memset(ybuf[:, :, 0:3], 0.0).then_inc(dve_step, 1)
            dve.wait_ge(dve_step, 1)
            for s, credit in ((bank_free, NB), (convolved, 2), (silu_done, 1)):
                dve.sem_inc(s, credit)
            steps = Steps(dve, dve_step)
            steps.n = 1
            h.make_columns(dve)
            h.make(dve, range(KC))
            dve.wait_ge(w_first, 16)
            for T in range(2):
                split(dve, T, wraw[:, :, T * P:(T + 1) * P], steps)
            h.make(dve, range(KC, NB * KC))
            dve.wait_ge(h.made, NB * KC)
            nc.vector.memset(sq[:, :], 1.0).then_inc(squared, 1)
            start = steps.n
            dve.wait_ge(taps_in, 16)
            with dve.Fori(0, QK_ITERS) as i:
                PER_ITER = TPI * 4
                steps.restart(i * PER_ITER + start)
                for t in range(TPI):
                    vector_tile(dve, i, i * TPI + t, t, True, True, steps)
                assert steps.n == PER_ITER
            steps.restart(QK_ITERS * PER_ITER + start)
            for T in range(QK_ITERS * TPI, ITERS * TPI):
                i, t = T // TPI, T % TPI
                convolve = i < QK_ITERS + V_ITERS
                if i < ITERS - 1 or t < 2:
                    vector_tile(dve, i, T, t, T == QK_ITERS * TPI, convolve, steps)
                elif t == 2:
                    dve.wait_ge(bank_full, T * NB + NB)
                    dve.wait_ge(ab_in, 16)
                    steps.did(nc.vector.memset(w_high[:, 0].bitcast(F32), 0.0))
                    steps.did(nc.vector.memset(w_low[:, 0].bitcast(F32), 0.0))
                    steps.wait()
                    split(dve, 0, wab[:, :, :], steps)

        def scalar_tile(act, T, slot, norm_before, kind, steps):
            if kind == "z":
                act.wait_ge(stored, 16 * (T + 1))
            elif kind != "ab":
                act.wait_ge(convolved, T + 1)
            for n in range(NB):
                act.wait_ge(bank_full, T * NB + (n + 1))
                out, f, rows = {"z": (sil[:, n * BLK:(n + 1) * BLK], ACT.Silu, P),
                                "ab": (acc[0:2 * AH, n * BLK:(n + 1) * BLK], ACT.Copy, 2 * AH)}\
                    .get(kind, (ybuf[:, slot, 3 + n * BLK:3 + (n + 1) * BLK], ACT.Copy, P))
                nc.scalar.activation(out, y[0:rows, n], f).then_inc(bank_free, 1)
            if norm_before:
                act.wait_ge(summed, T + 1)
                steps.did(nc.scalar.activation(sq[:, :], norm[:, :].rearrange("p a b -> p (a b)"), ACT.Ln, bias=eps[:, :]))
                steps.wait()
                nc.scalar.activation(sq[:, :], sq[:, :], ACT.Exp, scale=-0.5).then_inc(rooted, 1)
            if kind in ("z", "ab"):
                return
            act.wait_ge(convolved, T + 3)
            act.wait_ge(stored, 16 * (T + 1))
            nc.scalar.activation(sil[:, :], acc[:, :], ACT.Silu).then_inc(silu_done, 1)
            if kind == "qk":
                act.wait_ge(silu_done, T + 2)
                act.wait_ge(scaled, T + 1)
                nc.scalar.activation(sq[:, :], sil[:, :], ACT.Square).then_inc(squared, 1)

        @block.scalar
        def _(act):
            steps = Steps(act, act_step)
            h.scale(act)
            act.wait_ge(dve_step, 1)
            with act.Fori(0, QK_ITERS) as i:
                steps.restart(i * TPI)
                for t in range(TPI):
                    scalar_tile(act, i * TPI + t, t % 2, True, "qk", steps)
            steps.restart(QK_ITERS * TPI)
            for T in range(QK_ITERS * TPI, ITERS * TPI + 1):
                kind = "v" if T < (QK_ITERS + V_ITERS) * TPI else "z" if T < ITERS * TPI else "ab"
                if kind == "ab":
                    act.wait_ge(silu_done, (QK_ITERS + V_ITERS) * TPI + 1)
                scalar_tile(act, T, T % 2, T == QK_ITERS * TPI, kind, steps)

        @block.gpsimd
        def _(pool):
            with pool.Fori(0, QK_ITERS * TPI) as T:
                pool.wait_ge(scaled, T + 1)
                pool.dma_start(s_qkv[bass.ds(T * P, P), :], sil[:, :]).then_inc(stored, 16)
            T = QK_ITERS * TPI
            pool.wait_ge(scaled, T + 1)
            pool.dma_start(s_qkv[T * P:(T + 1) * P, :], sil[:, :]).then_inc(stored, 16)
            for T in range(QK_ITERS * TPI, (QK_ITERS + V_ITERS) * TPI):
                pool.wait_ge(silu_done, T + 2)
                pool.dma_start(s_qkv[(T + 1) * P:(T + 2) * P, :], sil[:, :]).then_inc(stored, 16)
            for T in range((QK_ITERS + V_ITERS) * TPI, ITERS * TPI):
                pool.wait_ge(bank_free, (T + 2) * NB)
                at = (T - (QK_ITERS + V_ITERS) * TPI) * P
                pool.dma_start(s_zT[at:at + P, :], sil[:, :]).then_inc(stored, 16)
            pool.wait_ge(bank_free, (ITERS * TPI + 2) * NB)
            pool.dma_start(s_abT[:, :], acc[0:2 * AH, :]).then_inc(stored, 16)
            pool.wait_ge(stored, 16 * (ITERS * TPI + 2))


class Event:

    def __init__(self, st, name, per=2, credit=0):
        self.sem, self.per, self.credit = st.sem(name), per, credit

    def wait(self, eng, rnd, part, back=0):
        value = rnd * self.per + (part + 1 + self.credit - back * self.per)
        assert not isinstance(value, int) or value > 0
        eng.wait_ge(self.sem, value)

    def done(self, ins):
        return ins.then_inc(self.sem, 1)

    def give_credit(self, eng):
        if self.credit:
            eng.sem_inc(self.sem, self.credit)


def over_heads(mask, n):
    return mask.unsqueeze(1).to_broadcast([P, n, P])


def delta_rule(nc, s_qkv, s_zT, s_abT, a_log, dt_bias, o_gain, level_masks, s_g, s_uT):
    C = P
    NC = SEQ // C
    HG = AH // 2
    LV = 7
    G_, GB_, BETA, NBEG, EKG, EGL = range(6)
    SCALE = float(P) ** -0.5
    with Stage(nc, "dr") as st:
        araw, braw = st.sb("araw", [AH, SEQ]), st.sb("braw", [AH, SEQ])
        atmp, btmp = st.sb("atmp", [AH, SEQ]), st.sb("btmp", [AH, SEQ])
        keep = st.sb("keep", [AH, SEQ])
        hcol = st.sb("hcol", [AH, 4])
        cols = st.sb("cols", [P, 6, NC, AH])
        ident, last_row = st.sb("ident", [P, P]), st.sb("last_row", [P, P])
        eps = st.sb("eps", [P, 1])
        gain = st.sb("gain", [P, 1])
        mask_a, mask_p = st.sb("mask_a", [P, P]), st.sb("mask_p", [P, P])
        levels = st.sb("levels", [P, LV, P], U8)
        qkv = [st.sb(f"qkv{s}", [P, 3 * AH, C]) for s in range(2)]
        z = [st.sb(f"z{s}", [P, AH, C]) for s in range(2)]
        gb = [st.sb(f"gb{s}", [P, AH, C]) for s in range(2)]
        arg_a, arg_p = st.sb("arg_a", [P, AH, C]), st.sb("arg_p", [P, AH, C])
        sd, sa = [st.sb(f"sd{s}", [P, 6, AH]) for s in range(2)], st.sb("sa", [P, 6, AH])
        q_hat, bv, k_hat = (st.sb(n, [P, AH, C]) for n in ("q_hat", "bv", "k_hat"))
        B, PT, T, TT, Z = (st.sb(n, [P, AH, C]) for n in ("B", "PT", "T", "TT", "Z"))
        R, VN, S, ON, U = (st.sb(n, [P, AH, C]) for n in ("R", "VN", "S", "ON", "U"))
        ss, rstd = st.sb("ss", [P, AH]), st.sb("rstd", [P, AH])
        psX, psZ, psT, psTT = (st.ps(n, [P, 2, BLK]) for n in ("psX", "psZ", "psT", "psTT"))

        consts_in, levels_set, ab_in = st.sem("consts_in"), st.sem("levels_set"), st.sem("ab_in")
        pool_set, dve_gates, act_gates, gates_stored = (st.sem(n) for n in ("pool_set", "dve_gates", "act_gates", "gates_stored"))
        turned, tables = st.sem("turned"), st.sem("tables")
        qkv_in, z_in, gb_in = ([st.sem(f"{n}{s}") for s in range(2)] for n in ("qkv_in", "z_in", "gb_in"))
        stored = [st.sem(f"stored{g}") for g in range(2)]
        dve_passed, pool_passed = st.sem("dve_passed"), st.sem("pool_passed")
        ev = lambda name, per=2, credit=0: Event(st, name, per, credit)
        scal_d, scal_a = ev("scal_d", 1), ev("scal_a", 1)
        args, decays, qh_ok, bv_ok, kh_ok = ev("args"), ev("decays"), ev("qh_ok"), ev("bv_ok"), ev("kh_ok")
        v_turned, k_turned, gram_ok, qk_ok = ev("v_turned"), ev("k_turned"), ev("gram_ok"), ev("qk_ok")
        b_ok, pt_ok = ev("b_ok"), ev("pt_ok")
        reset, z_ok, z_copied = ev("reset"), ev("z_ok", 2 * LV), ev("z_copied", 2 * (LV - 1))
        tt_ok, t_ok, t_copied = (ev(n, 2 * (LV - 1)) for n in ("tt_ok", "t_ok", "t_copied"))
        level_ok = ev("level_ok", 2 * LV)
        ks_ok, r_ok, tr_ok, vn_ok = ev("ks_ok"), ev("r_ok"), ev("tr_ok", credit=2), ev("vn_ok", credit=2)
        o_ok, st_ok, s_ok, squares, on_ok = ev("o_ok", credit=2), ev("st_ok"), ev("s_ok", credit=2), ev("squares"), ev("on_ok", credit=2)
        norm_step = ev("norm_step", 4)
        ot_ok, out_ok = ev("ot_ok", credit=2), ev("out_ok", credit=2)
        block = st.block()

        def group(g):
            return slice(g * HG, (g + 1) * HG)

        def flat(x, g):
            return x[:, group(g)].rearrange("p h c -> p (h c)")

        def heads(g):
            return range(g * HG, (g + 1) * HG)

        def at(ps, g, h):
            return ps[:, g, (h % HG) * C:(h % HG + 1) * C]

        def load(sp, c, s):
            tok = bass.ds(c * C, C)
            sp.dma_start(gb[s][:, :, :], s_g[:, tok].unsqueeze(0).to_broadcast([P, AH, C])).then_inc(gb_in[s], 16)
            sp.dma_start(qkv[s][:, :, :], s_qkv[P:, tok].rearrange("(t p) s -> p t s", p=P)).then_inc(qkv_in[s], 16)
            sp.dma_start(z[s][:, :, :], s_zT[:, tok].rearrange("(t p) s -> p t s", p=P)).then_inc(z_in[s], 16)

        def store(sp, c):
            for g in range(2):
                out_ok.wait(sp, c, g)
                sp.dma_start(s_uT[g * HG * P:(g + 1) * HG * P, bass.ds(c * C, C)].rearrange("(h p) s -> p h s", p=P),
                             U[:, group(g)]).then_inc(stored[g], 16)

        @block.sync
        def _(sp):
            sp.dma_start(araw[:, :], s_abT[0:AH, :]).then_inc(ab_in, 16)
            sp.dma_start(braw[:, :], s_abT[AH:2 * AH, :]).then_inc(ab_in, 16)
            sp.dma_start(hcol[:, 0:1], a_log).then_inc(ab_in, 16)
            sp.dma_start(hcol[:, 1:2], dt_bias).then_inc(ab_in, 16)
            sp.dma_start(gain[:, :], o_gain).then_inc(consts_in, 16)
            sp.dma_start(Z[:, 0:LV], level_masks).then_inc(consts_in, 16)
            sp.wait_ge(dve_gates, 6)
            sp.dma_start(s_g[:, :], araw[:, :]).then_inc(gates_stored, 16)
            sp.wait_ge(gates_stored, 16)
            for s in range(2):
                load(sp, s, s)
            for g in range(2):
                sp.sem_inc(stored[g], 16)
            with sp.Fori(0, NC // 2 - 1) as i:
                for s in range(2):
                    store(sp, i * 2 + s)
                    load(sp, i * 2 + (s + 2), s)
            for c in range(NC - 2, NC):
                store(sp, c)
            for g in range(2):
                sp.wait_ge(stored[g], 16 * (NC + 1))

        @block.gpsimd
        def _(pool):
            g = nc.gpsimd
            g.memset(ident[:, :], 0.0)
            g.memset(last_row[:, :], 0.0)
            g.memset(keep[:, :], 1.0)
            g.memset(eps[:, :], EPS)
            g.memset(mask_a[:, :], 0.0)
            g.memset(S[:, :, :], 0.0)
            g.memset(mask_p[:, :], 0.0).then_inc(pool_set, 1)
            pool.wait_ge(pool_set, 1)
            sel = lambda x, fill, op, base, step, mult: g.affine_select(
                out=x, in_=x, compare_op=op, fill=fill, base=base, pattern=[[step, P]], channel_multiplier=mult)
            sel(ident[:, :], 1.0, ALU.not_equal, 0, -1, 1)
            g.affine_select(out=last_row[:, :], in_=last_row[:, :], compare_op=ALU.not_equal, fill=1.0,
                            base=-(P - 1), pattern=[[0, P]], channel_multiplier=1)
            sel(mask_a[:, :], BIG, ALU.is_gt, 0, -1, 1)
            sel(mask_p[:, :], -BIG, ALU.is_ge, 0, 1, -1)
            g.memset(keep[:, 0:SEQ:C], 0.0).then_inc(pool_set, 1)
            for e in (tr_ok, vn_ok, s_ok, o_ok, on_ok, ot_ok, out_ok):
                e.give_credit(pool)
            pool.wait_ge(pool_set, 2)
            with pool.Fori(0, NC) as c:
                for q in range(2):
                    tr_ok.wait(pool, c, q, back=1)
                    pool.sem_inc(pool_passed, 1)
                    for h in heads(q):
                        ins = g.tensor_copy(TT[:, h], ident[:, :])
                    reset.done(ins)

        def gates_vector(dve):
            v = nc.vector
            steps = Steps(dve, dve_gates)
            dve.wait_ge(ab_in, 64)
            dve.wait_ge(pool_set, 2)
            steps.did(v.tensor_scalar(araw[:, :], araw[:, :], hcol[:, 1:2], None, ALU.add))
            steps.wait()
            steps.did(v.scalar_tensor_tensor(atmp[:, :], araw[:, :], -1.0, araw[:, :], ALU.mult, ALU.max))
            steps.did(v.scalar_tensor_tensor(btmp[:, :], braw[:, :], -1.0, braw[:, :], ALU.mult, ALU.max))
            dve.wait_ge(act_gates, 5)
            steps.did(v.scalar_tensor_tensor(atmp[:, :], araw[:, :], 0.0, atmp[:, :], ALU.max, ALU.add))
            steps.wait()
            steps.did(v.tensor_scalar(atmp[:, :], atmp[:, :], hcol[:, 2:3], -1.0, ALU.mult, ALU.mult))
            steps.wait()
            steps.did(v.tensor_tensor_scan(araw[:, :], keep[:, :], atmp[:, :], 0.0, ALU.mult, ALU.add))
            steps.did(v.scalar_tensor_tensor(btmp[:, :], braw[:, :], 0.0, btmp[:, :], ALU.min, ALU.subtract))
            dve.wait_ge(turned, 1)
            raw = psX[:, 0].rearrange("p (k c h) -> p k c h", k=4, h=AH)
            steps.did(v.tensor_copy(cols[:, G_], raw[:, 0]))
            steps.wait()
            steps.did(v.tensor_tensor(cols[:, GB_], raw[:, 1], cols[:, G_], ALU.add))
            steps.did(v.tensor_copy(cols[:, BETA], raw[:, 1]))
            dve.wait_ge(turned, 2)
            steps.did(v.tensor_tensor(cols[:, EKG], psX[:, 1, 0:NC * AH].rearrange("p (c h) -> p c h", h=AH), cols[:, G_], ALU.subtract))
            steps.did(v.tensor_copy(cols[:, EGL], psX[:, 1, 0:NC * AH].rearrange("p (c h) -> p c h", h=AH)))
            steps.wait()
            dve.sem_inc(tables, 1)
            dve.wait_ge(act_gates, 9)
            steps.did(v.tensor_scalar(cols[:, NBEG], cols[:, NBEG], -1.0, None, ALU.mult))
            steps.wait()
            dve.sem_inc(tables, 1)

        def gates_scalar(act):
            a = nc.scalar
            steps = Steps(act, act_gates)
            act.preload_act_table_set("natural_log_exp_and_others")
            act.wait_ge(ab_in, 64)
            act.wait_ge(pool_set, 2)
            steps.did(a.activation(hcol[:, 2:3], hcol[:, 0:1], ACT.Exp))
            act.wait_ge(dve_gates, 3)
            for x in (atmp, btmp):
                steps.did(a.activation(x[:, :], x[:, :], ACT.Exp, scale=-1.0))
                steps.wait()
                steps.did(a.activation(x[:, :], x[:, :], ACT.Ln, bias=1.0))
            act.wait_ge(tables, 1)
            steps.did(a.activation(cols[:, NBEG], cols[:, GB_], ACT.Exp))
            for k in (BETA, EKG, EGL):
                steps.did(a.activation(cols[:, k], cols[:, k], ACT.Exp))
            act.wait_ge(tables, 2)

        def gates_tensor(pe):
            pe.wait_ge(pool_set, 2)
            pe.wait_ge(dve_gates, 7)
            raw = psX[:, 0].rearrange("p (k c h) -> p k c h", k=4, h=AH)
            for k, x in ((0, araw), (1, btmp)):
                for c in range(NC):
                    ins = nc.tensor.transpose(raw[:, k, c], x[:, c * C:(c + 1) * C], ident[0:AH, 0:AH])
            ins.then_inc(turned, 1)
            pe.wait_ge(dve_gates, 8)
            nc.tensor.matmul(psX[:, 1, 0:NC * AH], last_row[:, :], cols[:, G_].rearrange("p c h -> p (c h)"),
                             start=True, stop=True).then_inc(turned, 1)
            pe.wait_ge(tables, 2)

        def tensor_chunk(pe, c, i, s, first, more):
            mm, tr = nc.tensor.matmul, nc.tensor.transpose
            q, k, v = (qkv[s][:, j * AH:(j + 1) * AH] for j in range(3))
            pe.wait_ge(qkv_in[s], i * 16 + 16)
            for g in range(2):
                vn_ok.wait(pe, c, g, back=1)
                for h in heads(g):
                    ins = mm(at(psZ, g, h), k[:, h], k[:, h], start=True, stop=True)
                gram_ok.done(ins)
            for g in range(2):
                s_ok.wait(pe, c, g, back=1)
                for h in heads(g):
                    ins = mm(at(psTT, g, h), k[:, h], q[:, h], start=True, stop=True)
                qk_ok.done(ins)
            for g in range(2):
                b_ok.wait(pe, c, g)
                for h in heads(g):
                    ins = tr(at(psZ, g, h), B[:, h], ident[:, :])
                z_ok.done(ins)
            if not first:
                turn_out(pe, c, 1)
            for l in range(1, LV):
                for g in range(2):
                    level_ok.wait(pe, c, 2 * (l - 1) + g)
                    for h in heads(g):
                        ins = mm(at(psZ, g, h), B[:, h], TT[:, h], start=True, stop=True)
                    z_ok.done(ins)
                    if l == 1:
                        on_ok.wait(pe, c, g, back=1)
                    for h in heads(g):
                        ins = tr(at(psT, g, h), TT[:, h], ident[:, :])
                    t_ok.done(ins)
                for g in range(2):
                    z_copied.wait(pe, c, 2 * (l - 1) + g)
                    t_copied.wait(pe, c, 2 * (l - 1) + g)
                    for h in heads(g):
                        ins = mm(at(psTT, g, h), T[:, h], Z[:, h], start=True, stop=True)
                    tt_ok.done(ins)
                if l == 1:
                    for g in range(2):
                        out_ok.wait(pe, c, g, back=1)
                        for h in heads(g):
                            ins = tr(at(psX, g, h), k[:, h], ident[:, :])
                        k_turned.done(ins)
                if l in (3, 4):
                    g = l - 3
                    kh_ok.wait(pe, c, g)
                    for h in heads(g):
                        ins = tr(at(psX, g, h), v[:, h], ident[:, :])
                    v_turned.done(ins)
            for g in range(2):
                bv_ok.wait(pe, c, g)
                for h in heads(g):
                    ins = mm(at(psX, g, h), k[:, h], S[:, h], start=True, stop=True)
                ks_ok.done(ins)
            for g in range(2):
                level_ok.wait(pe, c, 2 * (LV - 1) + g)
                r_ok.wait(pe, c, g)
                for h in heads(g):
                    ins = mm(at(psZ, g, h), TT[:, h], R[:, h], start=True, stop=True)
                tr_ok.done(ins)
            for g in range(2):
                kh_ok.wait(pe, c, g)
                vn_ok.wait(pe, c, g)
                for h in heads(g):
                    ins = mm(at(psTT, g, h), k_hat[:, h], VN[:, h], start=True, stop=True)
                st_ok.done(ins)
                qh_ok.wait(pe, c, g)
                for h in heads(g):
                    mm(at(psT, g, h), q_hat[:, h], S[:, h], start=True, stop=False)
                    ins = mm(at(psT, g, h), PT[:, h], VN[:, h], start=False, stop=True)
                o_ok.done(ins)
            if not more:
                turn_out(pe, c, 0)

        def turn_out(pe, c, back):
            for g in range(2):
                on_ok.wait(pe, c, g, back=back)
                for h in heads(g):
                    ins = nc.tensor.transpose(at(psX, g, h), ON[:, h], ident[:, :])
                ot_ok.done(ins)

        def arguments(dve, c, s, which):
            stt = nc.vector.scalar_tensor_tensor
            for h in which:
                stt(arg_a[:, h], gb[s][:, h], sd[s][:, GB_, h:h + 1], mask_a[:, :], ALU.subtract, ALU.add)
                ins = stt(arg_p[:, h], gb[s][:, h], sd[s][:, G_, h:h + 1], mask_p[:, :], ALU.subtract, ALU.add)
                if h % HG == HG - 1:
                    args.done(ins)

        def scalars(dve, c, s):
            scal_d.done(nc.vector.tensor_copy(sd[s][:, :, :], cols[:, :, bass.ds(c, 1)].rearrange("p k a h -> p k (a h)")))
            scal_d.wait(dve, c, 0)

        def gate_out(dve, c, i, s, back):
            dve.wait_ge(z_in[s], i * 16 + 16)
            for g in range(2):
                ot_ok.wait(dve, c, g, back=back)
                dve.wait_ge(stored[g], c * 16 + (1 - back) * 16)
                out_ok.done(nc.vector.scalar_tensor_tensor(flat(U, g), psX[:, g], gain[:, 0:1], flat(z[s], g), ALU.mult, ALU.mult))

        def vector_chunk(dve, c, i, s, first, more):
            v = nc.vector
            stt = v.scalar_tensor_tensor
            q = qkv[s][:, 0:AH]
            s_ok.wait(dve, c, 1, back=1)
            for g in range(2):
                gram_ok.wait(dve, c, g)
                decays.wait(dve, c, g)
                b_ok.done(stt(flat(B, g), psZ[:, g], -1.0, flat(arg_a, g), ALU.mult, ALU.mult))
            for g in range(2):
                qk_ok.wait(dve, c, g)
                pt_ok.done(stt(flat(PT, g), psTT[:, g], SCALE, flat(arg_p, g), ALU.mult, ALU.mult))
                z_ok.wait(dve, c, g)
                reset.wait(dve, c, g)
                b_ok.wait(dve, c, g)
                dve.sem_inc(dve_passed, 1)
                level_ok.done(v.copy_predicated(TT[:, group(g)], over_heads(levels[:, 0], HG),
                                                psZ[:, g].rearrange("p (h c) -> p h c", h=HG)))
            if not first:
                gate_out(dve, c, i if s else i - 1, 1 - s, 1)
            for l in range(1, LV):
                for g in range(2):
                    tt_ok.wait(dve, c, 2 * (l - 1) + g)
                    dve.sem_inc(dve_passed, 1)
                    level_ok.done(v.copy_predicated(TT[:, group(g)], over_heads(levels[:, l], HG),
                                                    psTT[:, g].rearrange("p (h c) -> p h c", h=HG)))
                if l == 1:
                    for g in range(2):
                        decays.wait(dve, c, g)
                        dve.wait_ge(qkv_in[s], i * 16 + 16)
                        o_ok.wait(dve, c, g, back=1)
                        qh_ok.done(stt(flat(q_hat, g), flat(q, g), SCALE, flat(gb[s], g), ALU.mult, ALU.mult))
                if l == 2 and more:
                    scalars(dve, c + 1, 1 - s)
                    pt_ok.wait(dve, c, 1)
                    dve.wait_ge(gb_in[1 - s], (i + s) * 16 + 16)
                if l in (2, 3, 4) and more:
                    arguments(dve, c + 1, 1 - s, range((l - 2) * 3, min(AH, (l - 1) * 3)))
                if l in (4, 5):
                    g = l - 4
                    v_turned.wait(dve, c, g)
                    for h in heads(g):
                        ins = v.tensor_scalar(bv[:, h], at(psX, g, h), sd[s][:, BETA, h:h + 1], None, ALU.mult)
                    bv_ok.done(ins)
            for g in range(2):
                ks_ok.wait(dve, c, g)
                bv_ok.wait(dve, c, g)
                for h in heads(g):
                    ins = stt(R[:, h], at(psX, g, h), sd[s][:, NBEG, h:h + 1], bv[:, h], ALU.mult, ALU.add)
                r_ok.done(ins)
            for g in range(2):
                o_ok.wait(dve, c, g)
                s_ok.wait(dve, c, g, back=1)
                for h in heads(g):
                    ins = stt(S[:, h], S[:, h], sd[s][:, EGL, h:h + 1], at(psTT, g, h), ALU.mult, ALU.add)
                s_ok.done(ins)
            if not more:
                gate_out(dve, c, i, s, 0)

        def exponentials(act, c, s, g):
            a = nc.scalar
            args.wait(act, c, g)
            a.activation(flat(arg_a, g), flat(arg_a, g), ACT.Exp, scale=-1.0)
            a.activation(flat(arg_p, g), flat(arg_p, g), ACT.Exp)
            decays.done(a.activation(flat(gb[s], g), flat(gb[s], g), ACT.Exp))

        def scalar_chunk(act, c, i, s, first, more):
            a = nc.scalar
            on_ok.wait(act, c, 1, back=1)
            scal_a.done(a.activation(sa[:, :, :], cols[:, :, bass.ds(c, 1)].rearrange("p k a h -> p k (a h)"), ACT.Copy))
            for l in range(1, LV):
                for g in range(2):
                    z_ok.wait(act, c, 2 * l + g)
                    z_copied.done(a.activation(flat(Z, g), psZ[:, g], ACT.Copy))
                    t_ok.wait(act, c, 2 * (l - 1) + g)
                    t_copied.done(a.activation(flat(T, g), psT[:, g], ACT.Copy))
                if l in (2, 3):
                    g = l - 2
                    scal_a.wait(act, c, 0)
                    k_turned.wait(act, c, g)
                    for h in heads(g):
                        ins = a.activation(k_hat[:, h], at(psX, g, h), ACT.Copy, scale=sa[:, EKG, h:h + 1])
                    kh_ok.done(ins)
                if l in (4, 5) and more:
                    exponentials(act, c + 1, 1 - s, l - 4)
            for g in range(2):
                tr_ok.wait(act, c, g)
                vn_ok.done(a.activation(flat(VN, g), psZ[:, g], ACT.Copy))
            for g in range(2):
                o_ok.wait(act, c, g)
                for h in heads(g):
                    ins = a.activation(ON[:, h], at(psT, g, h), ACT.Square, accum_out=ss[:, h:h + 1])
                squares.done(ins)
                squares.wait(act, c, g)
                norm_step.done(a.activation(ss[:, group(g)], ss[:, group(g)], ACT.Ln, bias=eps[:, :], scale=1.0 / P))
                norm_step.wait(act, c, 2 * g)
                norm_step.done(a.activation(rstd[:, group(g)], ss[:, group(g)], ACT.Exp, scale=-0.5))
                norm_step.wait(act, c, 2 * g + 1)
                for h in heads(g):
                    ins = a.activation(ON[:, h], at(psT, g, h), ACT.Copy, scale=rstd[:, h:h + 1])
                on_ok.done(ins)

        def over_chunks(eng, body):
            for c in range(2):
                body(eng, c, 0, c, c == 0, True)
            with eng.Fori(1, NC // 2 - 1) as i:
                for s in range(2):
                    body(eng, i * 2 + s, i, s, False, True)
            for c in range(NC - 2, NC):
                body(eng, c, c // 2, c % 2, False, c < NC - 1)

        @block.tensor
        def _(pe):
            gates_tensor(pe)
            over_chunks(pe, tensor_chunk)

        @block.vector
        def _(dve):
            gates_vector(dve)
            dve.wait_ge(consts_in, 32)
            nc.vector.tensor_copy(levels[:, :], Z[:, 0:LV]).then_inc(levels_set, 1)
            dve.wait_ge(levels_set, 1)
            scalars(dve, 0, 0)
            dve.wait_ge(gb_in[0], 16)
            arguments(dve, 0, 0, range(AH))
            over_chunks(dve, vector_chunk)

        @block.scalar
        def _(act):
            gates_scalar(act)
            act.wait_ge(gb_in[0], 16)
            for g in range(2):
                exponentials(act, 0, 0, g)
            over_chunks(act, scalar_chunk)


def output_projection(nc, name, s_uT, w_out, s_mod, gate_at, post_g, x, x_out, s_xnT):
    WS = 4
    with Stage(nc, name) as st:
        ident, eps = st.sb("ident", [P, P]), st.sb("eps", [P, 1])
        w_high, w_low = st.sb("w_high", [P, KC, D], F32R), st.sb("w_low", [P, KC, D], F32R)
        wraw = st.sb("wraw", [P, WS, D])
        gate, post = st.sb("gate", [P, D]), st.sb("post", [P, D])
        u = st.sb("u", [P, 2, KC, P])
        u_high, u_low = st.sb("u_high", [P, 2, KC, P], F32R), st.sb("u_low", [P, 2, KC, P], F32R)
        xt, xo, xn, xT = (st.sb(n, [P, 2, D]) for n in ("xt", "xo", "xn", "xT"))
        junk = st.sb("junk", [P, 2, D])
        ss = st.sb("ss", [P, 4, 1])
        y, turned = st.ps("y", [P, 2, D]), st.ps("turned", [P, 2, D])
        x_stored, t_stored = ([st.sem(f"{n}{s}") for s in range(2)] for n in ("x_stored", "t_stored"))
        w_in = [st.sem(f"w_in{s}") for s in range(WS)]
        u_in, x_in = ([st.pool_sem(f"{n}{s}") for s in range(2)] for n in ("u_in", "x_in"))
        rows_in = st.pool_sem("rows_in")
        ident_ok, step, act_step, w_split = (st.sem(n) for n in ("ident_ok", "step", "act_step", "w_split"))
        sp_passed, w_rounded = st.sem("sp_passed"), st.sem("w_rounded")
        ev = lambda n, per=1, credit=0: Event(st, n, per, credit)
        u_split, y_ok, r_ok, out_ok = ev("u_split"), ev("y_ok", credit=2), ev("r_ok"), ev("out_ok", credit=2)
        r2_ok, xn_ok, turned_ok, xT_ok = ev("r2_ok"), ev("xn_ok"), ev("turned_ok", credit=2), ev("xT_ok", credit=2)
        block = st.block()

        def loop(eng, body):
            with eng.Fori(0, NT // 2 - 1) as i:
                for s in range(2):
                    body(i * 2 + s, i, s, False)
            for c in range(NT - 2, NT):
                body(c, c // 2, c % 2, True)

        @block.gpsimd
        def _(pool):
            def load(c, s):
                pool.dma_start(u[:, s], s_uT.rearrange("(k p) t -> p k t", p=P)[:, :, bass.ds(c * P, P)]).then_inc(u_in[s], 16)
                pool.dma_start(xt[:, s], x[bass.ds(c * P, P), :]).then_inc(x_in[s], 16)

            for s in range(2):
                load(s, s)
            pool.dma_start(gate[:, :], s_mod[:, gate_at:gate_at + D].to_broadcast([P, D])).then_inc(rows_in, 16)
            pool.dma_start(post[:, :], post_g.to_broadcast([P, D])).then_inc(rows_in, 16)
            make_identity(pool, ident[:, :], ident_ok)
            nc.gpsimd.memset(eps[:, :], EPS).then_inc(ident_ok, 1)
            with pool.Fori(0, NT // 2 - 1) as i:
                for s in range(2):
                    out_ok.wait(pool, i * 2 + s, 0)
                    load(i * 2 + (s + 2), s)

        @block.sync
        def _(sp):
            for k in range(KC):
                if k >= WS:
                    sp.wait_ge(w_split, k - WS + 1)
                sp.dma_start(wraw[:, k % WS], w_out[k * P:(k + 1) * P, :]).then_inc(w_in[k % WS], 16)
            for s in range(2):
                sp.sem_inc(x_stored[s], 16)
                sp.sem_inc(t_stored[s], 16)

            def store(c, i, s, last):
                out_ok.wait(sp, c, 0)
                sp.sem_inc(sp_passed, 1)
                sp.dma_start(x_out[bass.ds(c * P, P), :], xo[:, s]).then_inc(x_stored[s], 16)
                if s_xnT is not None:
                    xT_ok.wait(sp, c, 0)
                    sp.sem_inc(sp_passed, 1)
                    sp.dma_start(s_xnT.rearrange("(k p) t -> p k t", p=P)[:, :, bass.ds(c * P, P)],
                                 xT[:, s].rearrange("p (k t) -> p k t", k=KC)).then_inc(t_stored[s], 16)

            loop(sp, store)
            for s in range(2):
                sp.wait_ge(x_stored[s], 16 * (NT // 2 + 1))
                if s_xnT is not None:
                    sp.wait_ge(t_stored[s], 16 * (NT // 2 + 1))

        def project(pe, c, s, first=False):
            u_split.wait(pe, c, 0)
            out_ok.wait(pe, c, 0, back=2)
            for k in range(KC):
                if first:
                    pe.wait_ge(w_split, k + 1)
                for w, x in ((u_high, w_high), (u_high, w_low), (u_low, w_high)):
                    for half in range(2):
                        at = slice(half * BLK, (half + 1) * BLK)
                        ins = nc.tensor.matmul(y[:, s, at], w[:, s, k], x[:, k, at], start=k == 0 and w is u_high and x is w_high,
                                               stop=k == KC - 1 and w is u_low)
            y_ok.done(ins)

        @block.tensor
        def _(pe):
            project(pe, 0, 0, True)
            pe.wait_ge(ident_ok, 3)

            def body(c, i, s, last):
                if not (last and s == 1):
                    project(pe, c + 1, 1 - s)
                if s_xnT is not None:
                    xn_ok.wait(pe, c, 0)
                    xT_ok.wait(pe, c, 0, back=2)
                    for k in range(KC):
                        ins = nc.tensor.transpose(turned[:, s, k * P:(k + 1) * P], xn[:, s, k * P:(k + 1) * P], ident[:, :])
                    turned_ok.done(ins)

            loop(pe, body)

        @block.vector
        def _(dve):
            v = nc.vector
            steps = Steps(dve, step)
            for e in (y_ok, out_ok, turned_ok, xT_ok):
                e.give_credit(dve)

            def split(c, i, s):
                dve.wait_ge(u_in[s], i * 16 + 16)
                steps.did(v.tensor_copy(u_high[:, s], u[:, s]))
                steps.wait()
                u_split.done(v.tensor_tensor(u_low[:, s], u[:, s], u_high[:, s].bitcast(F32), ALU.subtract))

            split(0, 0, 0)
            split(1, 0, 1)
            for k in range(KC):
                dve.wait_ge(w_rounded, k + 1)
                v.tensor_tensor(w_low[:, k], wraw[:, k % WS], w_high[:, k].bitcast(F32), ALU.subtract).then_inc(w_split, 1)
            dve.wait_ge(rows_in, 32)
            steps.did(v.tensor_tensor(gate[:, :], gate[:, :], post[:, :], ALU.mult))
            steps.wait()
            start = steps.n
            PER = 2

            def body(c, i, s, last):
                steps.restart(c * PER + start)
                y_ok.wait(dve, c, 0)
                r_ok.wait(dve, c, 0)
                dve.wait_ge(x_stored[s], i * 16 + 16)
                steps.did(v.scalar_tensor_tensor(xo[:, s], y[:, s], ss[:, s], gate[:, :], ALU.mult, ALU.mult))
                dve.wait_ge(x_in[s], i * 16 + 16)
                steps.wait()
                out_ok.done(v.tensor_tensor(xo[:, s], xo[:, s], xt[:, s], ALU.add))
                if s_xnT is not None:
                    r2_ok.wait(dve, c, 0)
                    turned_ok.wait(dve, c, 0, back=2)
                    xn_ok.done(v.tensor_scalar(xn[:, s], xo[:, s], ss[:, 2 + s], None, ALU.mult))
                if not last:
                    y_ok.wait(dve, c, 0)
                    split(c + 2, i + 1, s)
                else:
                    dve.sem_inc(step, 1)
                    steps.n += 1
                if s_xnT is not None:
                    turned_ok.wait(dve, c, 0)
                    dve.wait_ge(t_stored[s], i * 16 + 16)
                    xT_ok.done(v.tensor_copy(xT[:, s], turned[:, s]))
                assert steps.n == PER

            loop(dve, body)

        @block.scalar
        def _(act):
            a = nc.scalar
            for k in range(KC):
                act.wait_ge(w_in[k % WS], 16 * (k // WS + 1))
                a.activation(w_high[:, k], wraw[:, k % WS], ACT.Copy).then_inc(w_rounded, 1)
            act.wait_ge(ident_ok, 3)
            act.preload_act_table_set("natural_log_exp_and_others")
            steps = Steps(act, act_step)
            per = 4 if s_xnT is not None else 2

            def root(src, col, event, c):
                steps.did(a.activation(junk[:, col // 2], src, ACT.Square, accum_out=ss[:, col]))
                steps.wait()
                steps.did(a.activation(ss[:, col], ss[:, col], ACT.Ln, bias=eps[:, :], scale=1.0 / D))
                steps.wait()
                event.done(a.activation(ss[:, col], ss[:, col], ACT.Exp, scale=-0.5))

            def body(c, i, s, last):
                steps.restart(c * per)
                y_ok.wait(act, c, 0)
                out_ok.wait(act, c, 0, back=2)
                root(y[:, s], s, r_ok, c)
                if s_xnT is not None:
                    out_ok.wait(act, c, 0)
                    turned_ok.wait(act, c, 0, back=2)
                    root(xo[:, s], 2 + s, r2_ok, c)

            loop(act, body)


def plain_projection(nc, name, s_xnT, s_mod, gain, shift_at, scale_at, w, first_scale, s_split, second, s_second,
                     gates=None, finish=None):
    TPI = 4
    ITERS = 2 * D // P // TPI
    TILES = ITERS * TPI
    HALF = TILES // 2
    by_token = second == "by token"
    with Stage(nc, name) as st:
        obuf = st.sb("obuf", [P, 2, SEQ])
        parts = st.sb("parts", [P, 2, SEQ], F32R)
        h = Modulated(st, s_xnT, s_mod, gain, shift_at, scale_at, [obuf[:, b, n * BLK:(n + 1) * BLK] for b in range(2) for n in range(NB)])
        wraw = st.sb("wraw", [P, KC, TPI * P])
        w_high, w_low = st.sb("w_high", [P, 2, KC, P], F32R), st.sb("w_low", [P, 2, KC, P], F32R)
        wg = st.sb("wg", [P, KC, BH])
        bias, ones = st.sb("bias", [BH, 1]), st.sb("ones", [BH, 1])
        ident = st.sb("ident", [P, P])
        y, turned = st.ps("y", [P, NB, BLK]), st.ps("turned", [P, NB, BLK])
        w_first, w_in, g_in = (st.pool_sem(n) for n in ("w_first", "w_in", "g_in"))
        ident_ok, w_split = st.sem("ident_ok"), st.sem("w_split")
        bank_full, bank_free, turned_ok, copied = (st.sem(n) for n in ("bank_full", "bank_free", "turned_ok", "copied"))
        parts_ok, dve_step, act_step, abs_ok = (st.sem(n) for n in ("parts_ok", "dve_step", "act_step", "abs_ok"))
        stored = [st.sem(f"stored{s}") for s in range(2)]
        x, e = (parts[0:BH, n].bitcast(F32) for n in range(2))
        p_stored, gates_stored, gates_ok, raw_in = (st.sem(n) for n in ("p_stored", "gates_stored", "gates_ok", "raw_in"))
        block = st.block()

        def weights(i):
            return w[:, bass.ds(i * (TPI * P), TPI * P)].rearrange("(k p) f -> p k f", p=P)

        @block.gpsimd
        def _(pool):
            pool.dma_start(wraw[:, :, 0:2 * P], weights(0)[:, :, 0:2 * P]).then_inc(w_first, 16)
            pool.wait_ge(h.made, KC)
            pool.dma_start(wraw[:, :, 2 * P:], weights(0)[:, :, 2 * P:]).then_inc(w_in, 16)
            if gates:
                pool.dma_start(wg[:, :, :], w[:, 2 * D:2 * D + BH].rearrange("(k p) f -> p k f", p=P)).then_inc(g_in, 16)
                pool.dma_start(bias[:, :], gates[0]).then_inc(g_in, 16)
            make_identity(pool, ident[:, :], ident_ok)
            with pool.Fori(1, ITERS) as i:
                pool.wait_ge(w_split, i * TPI)
                pool.dma_start(wraw[:, :, :], weights(i)).then_inc(w_in, 16)

        @block.sync
        def _(sp):
            sp.sem_inc(p_stored, 64)
            for s in range(2):
                sp.sem_inc(stored[s], 16)
            h.load_columns(sp)
            h.load(sp, range(NB * KC))
            for T in range(HALF):
                sp.wait_ge(parts_ok, T + 3)
                for a in range(2):
                    for low in range(2):
                        at = (2 * T + a) * P + (1 - low) * DH
                        sp.dma_start(s_split[at:at + DH, :], parts[a * DH:(a + 1) * DH, low].bitcast(F32)).then_inc(p_stored, 16)
            if finish:
                sp.wait_ge(p_stored, 64 * (HALF + 1))
                sp.dma_start(parts[0:BH, 0].bitcast(F32), finish[0]).then_inc(raw_in, 16)
            for i in range(TILES - HALF):
                if by_token:
                    sp.wait_ge(copied, i + 1)
                    sp.dma_start(s_second[:, i * P:(i + 1) * P].rearrange("(n t) f -> t n f", t=P),
                                 parts[:, i % 2].bitcast(F32).rearrange("t (n f) -> t n f", f=P)).then_inc(stored[i % 2], 16)
                else:
                    sp.wait_ge(bank_free, (HALF + i + 2) * NB)
                    sp.dma_start(s_second[i * P:(i + 1) * P, :], obuf[:, i % 2]).then_inc(stored[i % 2], 16)
            sp.wait_ge(p_stored, 64 * (HALF + 1))
            for s in range(2):
                sp.wait_ge(stored[s], 16 * (HALF // 2 + 1))
            if gates:
                sp.wait_ge(bank_free, (TILES + 2) * NB)
                sp.dma_start(gates[1], obuf[0:BH, 0]).then_inc(gates_stored, 16)
                sp.wait_ge(gates_stored, 16)
            if finish:
                sp.wait_ge(gates_ok, 6)
                for b in range(2):
                    sp.dma_start(finish[1][:, b, :], parts[0:BH, 1 - b].bitcast(F32)).then_inc(gates_stored, 16)
                sp.wait_ge(gates_stored, 32)

        def tensor_tile(pe, T, slot):
            pe.wait_ge(w_split, T + 1)
            for n in range(NB):
                pe.wait_ge(h.made, (n + 1) * KC)
                pe.wait_ge(bank_free, T * NB + (n + 1))
                three_passes(nc, y[:, n], w_high[:, slot], w_low[:, slot], h.high[:, :, n * BLK:(n + 1) * BLK],
                             h.low[:, :, n * BLK:(n + 1) * BLK]).then_inc(bank_full, 1)

        def turn(pe, T):
            pe.wait_ge(bank_free, (T + 2) * NB)
            if T > HALF:
                pe.wait_ge(copied, T - HALF)
            for n in range(NT):
                ins = nc.tensor.transpose(turned[:, n // 4, (n % 4) * P:(n % 4 + 1) * P],
                                          obuf[:, T % 2, n * P:(n + 1) * P], ident[:, :])
            ins.then_inc(turned_ok, 1)

        @block.tensor
        def _(pe):
            pe.wait_ge(ident_ok, 2)
            with pe.Fori(0, HALF // 2) as i:
                for t in range(2):
                    tensor_tile(pe, i * 2 + t, t)
            for T in range(HALF, TILES + (1 if gates else 0)):
                tensor_tile(pe, T, T % 2)
                if by_token and T > HALF:
                    turn(pe, T - 1)

        def split(dve, slot, raw, steps):
            steps.did(nc.vector.tensor_copy(w_high[:, slot, :, 0:raw.shape[2]], raw))
            steps.wait()
            nc.vector.tensor_tensor(w_low[:, slot, :, 0:raw.shape[2]], raw,
                                    w_high[:, slot, :, 0:raw.shape[2]].bitcast(F32), ALU.subtract).then_inc(w_split, 1)

        def split_next(dve, i, T, t, steps):
            dve.wait_ge(bank_full, T * NB + NB)
            dve.wait_ge(w_in, i * 16 + (32 if t >= 2 else 16))
            at = (t + 2) % TPI * P
            split(dve, t % 2, wraw[:, :, at:at + P], steps)

        def copy_turned(dve, T):
            i = T - HALF
            dve.wait_ge(turned_ok, i + 1)
            dve.wait_ge(stored[i % 2], 16 * (i // 2) + 16)
            dve.wait_ge(p_stored, 64 * (HALF + 1))
            nc.vector.tensor_copy(parts[:, i % 2].bitcast(F32), turned[:, :].rearrange("p a b -> p (a b)")).then_inc(copied, 1)

        @block.vector
        def _(dve):
            v = nc.vector
            dve.sem_inc(bank_free, NB)
            dve.sem_inc(parts_ok, 2)
            steps = Steps(dve, dve_step)
            h.make_columns(dve)
            h.make(dve, range(KC))
            dve.wait_ge(w_first, 16)
            for T in range(2):
                split(dve, T, wraw[:, :, T * P:(T + 1) * P], steps)
            h.make(dve, range(KC, NB * KC))
            start = steps.n
            PER_ITER = TPI * 2
            with dve.Fori(0, ITERS // 2) as i:
                steps.restart(i * PER_ITER + start)
                for t in range(TPI):
                    T = i * TPI + t
                    split_next(dve, i, T, t, steps)
                    dve.wait_ge(bank_free, T * NB + 2 * NB)
                    dve.wait_ge(p_stored, T * 64 + 64)
                    steps.did(v.tensor_copy(parts[:, 0], obuf[:, t % 2]))
                    steps.wait()
                    v.tensor_tensor(parts[:, 1], obuf[:, t % 2], parts[:, 0].bitcast(F32), ALU.subtract).then_inc(parts_ok, 1)
                assert steps.n == PER_ITER
            steps.restart(ITERS // 2 * PER_ITER + start)
            for T in range(HALF, TILES):
                if T < TILES - 2:
                    split_next(dve, T // TPI, T, T % TPI, steps)
                elif gates and T == TILES - 2:
                    dve.wait_ge(bank_full, T * NB + NB)
                    dve.wait_ge(g_in, 32)
                    steps.did(v.memset(w_high[:, 0].bitcast(F32), 0.0))
                    steps.did(v.memset(w_low[:, 0].bitcast(F32), 0.0))
                    steps.wait()
                    split(dve, 0, wg[:, :, :], steps)
                if by_token and T > HALF:
                    copy_turned(dve, T - 1)
                if finish and T == HALF + 1:
                    dve.wait_ge(raw_in, 16)
                    v.memset(ones[:, :], 1.0).then_inc(gates_ok, 1)
                    v.scalar_tensor_tensor(e, x, -1.0, x, ALU.mult, ALU.max).then_inc(abs_ok, 1)
                if finish and T == HALF + 4:
                    dve.wait_ge(act_step, 2)
                    v.tensor_scalar(x, x, 0.0, None, ALU.min).then_inc(gates_ok, 1)
                    dve.wait_ge(gates_ok, 2)
                    v.tensor_tensor(e, e, x, ALU.subtract).then_inc(gates_ok, 1)
                    dve.wait_ge(gates_ok, 3)
                    v.tensor_tensor_scan(x, ones[:, 0:1].to_broadcast([BH, SEQ]), e, 0.0, ALU.mult, ALU.add).then_inc(gates_ok, 1)
                    dve.wait_ge(gates_ok, 4)
                    v.tensor_copy(parts[0:BH, 1], x).then_inc(gates_ok, 1)
                    dve.wait_ge(gates_ok, 5)
                    v.tensor_tensor(parts[0:BH, 0], x, e, ALU.subtract).then_inc(gates_ok, 1)
            if by_token:
                copy_turned(dve, TILES - 1)

        @block.scalar
        def _(act):
            a = nc.scalar

            def evacuate(T, slot, func, scale, rows=P, **more):
                for n in range(NB):
                    act.wait_ge(bank_full, T * NB + (n + 1))
                    a.activation(obuf[0:rows, slot, n * BLK:(n + 1) * BLK], y[0:rows, n], func, scale=scale, **more)\
                     .then_inc(bank_free, 1)

            h.scale(act)
            act.wait_ge(h.made, NB * KC)
            with act.Fori(0, HALF // 2) as i:
                for t in range(2):
                    act.wait_ge(parts_ok, i * 2 + (t + 1))
                    evacuate(i * 2 + t, t, ACT.Copy, first_scale)
            for T in range(HALF, TILES):
                i = T - HALF
                act.wait_ge(parts_ok, min(T, HALF + 1) + 1)
                if by_token and i >= 2:
                    act.wait_ge(turned_ok, i - 1)
                if not by_token:
                    act.wait_ge(stored[T % 2], 16 * (i // 2) + 16)
                evacuate(T, T % 2, ACT.Copy if by_token else ACT.Silu, 1.0)
                if finish and T == HALF + 2:
                    act.wait_ge(abs_ok, 1)
                    a.activation(e, e, ACT.Exp, scale=-1.0).then_inc(act_step, 1)
                    act.wait_ge(act_step, 1)
                    a.activation(e, e, ACT.Ln, bias=1.0).then_inc(act_step, 1)
            if gates:
                act.wait_ge(turned_ok, HALF - 1)
                act.wait_ge(g_in, 32)
                evacuate(TILES, 0, ACT.Identity, 1.0, BH, bias=bias[:, :])


def attention(nc, s_K, s_Fp, s_V, s_Q, s_ZT, s_u2T):
    PAIRS = BH // 2
    NQ = BLK // P
    MAIN = [(qb, kb) for qb in reversed(range(NB)) for kb in range(NQ * (qb + 1))]
    MAXI = [(qb, h, sub, grp) for qb in range(NB) for h in range(2) for sub in range(NQ) for grp in range(qb + 1)]
    STEPS, MAXS = len(MAIN), len(MAXI)
    ENDS = [j for j in range(STEPS) if j == STEPS - 1 or MAIN[j][0] != MAIN[j + 1][0]]
    ON_POOL = [(j, h) for j in range(STEPS) for h in range(2) if MAIN[j][0] and MAIN[j][1] % 2]
    ON_DVE = [(j, h) for j in range(STEPS) for h in range(2) if (j, h) not in ON_POOL]
    MAX_START, MAX_END = 2, STEPS - 6
    with Stage(nc, "at") as st:
        K1, Q1, K2, Q2 = ([st.sb(f"{n}{s}", [P, 2, SEQ], F32R) for s in range(2)] for n in ("K1", "Q1", "K2", "Q2"))
        V = [st.sb(f"V{s}", [P, NT, P]) for s in range(2)]
        Z = [st.sb(f"Z{s}", [P, SEQ]) for s in range(2)]
        ident, ident_b, ones = st.sb("ident", [P, P]), st.sb("ident_b", [P, P], BF16), st.sb("ones", [P, DH])
        mask_q, mask_k = st.sb("mask_q", [P, P], BF16), st.sb("mask_k", [P, P], BF16)
        probs = st.sb("probs", [P, 3, 2, BLK])
        sum_v, sum_g = st.sb("sum_v", [P, 2, 2, BLK]), st.sb("sum_g", [P, 2, BLK])
        partial = st.sb("partial", [P, 2, NT, NB])
        top = st.sb("top", [P, 2 * NT])
        minus_top = st.sb("minus_top", [2 * NT, P], F32R)
        inv, u = st.sb("inv", [P, BLK]), st.sb("u", [P, 2, BLK])
        logits, rough = st.ps("logits", [P, 2, BLK]), st.ps("rough", [P, 2, BLK])
        o = st.ps("o", [P, 2, BLK])
        total, top_turned = st.ps("total", [P, BLK]), st.ps("top_turned", [P, BLK])
        one_in, two_in = ([[st.sem(f"{n}{s}{b}") for b in range(NB)] for s in range(2)] for n in ("one_in", "two_in"))
        u_stored = [st.sem(f"u_stored{s}") for s in range(2)]
        top_in = st.pool_sem("top_in")
        consts, sp_passed, pool_passed = (st.sem(n) for n in ("consts", "sp_passed", "pool_passed"))
        rows_set = [st.sem(f"rows_set{s}") for s in range(2)]
        ev = lambda n, per, credit=0: Event(st, n, per, credit)
        logits_ok, probs_ok, pv_ok = ev("logits_ok", 2 * STEPS), ev("probs_ok", 2 * STEPS, 2), ev("pv_ok", STEPS, 3)
        v_summed, g_summed = ev("v_summed", len(ON_DVE), 6), ev("g_summed", len(ON_POOL))
        joined, total_ok = ev("joined", 2 * (NB - 1), 2), ev("total_ok", NB, 2)
        logged, inv_ok = ev("logged", NB), ev("inv_ok", NB)
        rough_ok, reduced = ev("rough_ok", MAXS), ev("reduced", MAXS, 2)
        top_ok, top_turned_ok, minus_ok = ev("top_ok", 1, 1), ev("top_turned_ok", 1), ev("minus_ok", 1, 1)
        gated, u_ok = ev("gated", NB, 2), ev("u_ok", NB, 1)
        block = st.block()
        ONE, TWO = 3 * 16, 5 * 16

        def over_pairs(eng, body):
            with eng.Fori(0, PAIRS // 2 - 1) as i:
                for s in range(2):
                    body(i * 2 + s, i, s, True)
            for p in range(PAIRS - 2, PAIRS):
                body(p, p // 2, p % 2, p < PAIRS - 1)

        def late(j, lag):
            return [m for m, end in enumerate(ENDS) if end + lag == j]

        def width_from(j):
            qb, kb = MAIN[j]
            return max(0, kb - qb * NQ) * P

        @block.gpsimd
        def _(pool):
            g = nc.gpsimd
            g.memset(ident[:, :], 0.0)
            g.memset(ident_b[:, :], 0.0)
            g.memset(mask_q[:, :], 0.0)
            g.memset(mask_k[:, :], 0.0)
            g.memset(ones[:, :], 1.0)
            g.memset(partial[:, :, :, :], -BIG).then_inc(consts, 1)
            pool.wait_ge(consts, 1)
            sel = lambda x, fill, op, step, mult: g.affine_select(
                out=x[:, :], in_=x[:, :], compare_op=op, fill=fill, base=0, pattern=[[step, P]], channel_multiplier=mult)
            sel(ident, 1.0, ALU.not_equal, -1, 1)
            sel(ident_b, 1.0, ALU.not_equal, -1, 1)
            sel(mask_q, -BIG, ALU.is_ge, -1, 1)
            sel(mask_k, -BIG, ALU.is_ge, 1, -1).then_inc(consts, 1)
            pool.wait_ge(consts, 2)
            for x in (K1, Q1):
                g.memset(x[1][DH:DH + 3].bitcast(F32), 1.0).then_inc(rows_set[1], 1)
            pool.wait_ge(rows_set[1], 2)
            for e in (probs_ok, pv_ok, v_summed, joined, total_ok, reduced, top_ok, minus_ok, gated, u_ok):
                e.give_credit(pool)
            for s in range(2):
                pool.sem_inc(u_stored[s], 16)

            def place(p, s):
                minus_ok.wait(pool, p, 0)
                pool.sem_inc(pool_passed, 1)
                for h in range(2):
                    pool.dma_start(Q1[s][DH + 2:DH + 3, h].bitcast(F32), minus_top[h * NT:(h + 1) * NT].bitcast(F32))\
                        .then_inc(top_in, 16)

            def body(p, i, s, more):
                for j in range(STEPS):
                    qb, kb = MAIN[j]
                    m = NB - 1 - qb
                    for h in range(2):
                        if (j, h) in ON_POOL:
                            at = ON_POOL.index((j, h))
                            off = width_from(j)
                            probs_ok.wait(pool, p, 2 * j + h)
                            x = probs[:, j % 3, h, off:BLK]
                            if kb == 1:
                                joined.wait(pool, p, 2 * m + h - 2)
                                pool.sem_inc(pool_passed, 1)
                                ins = g.tensor_copy(sum_g[:, h], x)
                            else:
                                g_summed.wait(pool, p, at - 2)
                                ins = g.tensor_tensor(sum_g[:, h, off:BLK], sum_g[:, h, off:BLK], x, ALU.add)
                            g_summed.done(ins)
                    if more and j == MAX_END + 3:
                        place(p + 1, 1 - s)

            place(0, 0)
            over_pairs(pool, body)

        def sources(p, n):
            return [x[bass.ds(p * (2 * P), 2 * P), n * BLK:(n + 1) * BLK].rearrange("(h w d) t -> w d h t", h=2, w=2)
                    for x in (s_K, s_Q)]

        def load_one(sp, p, s, n):
            at = slice(n * BLK, (n + 1) * BLK)
            for to, of in zip((K1, Q1), sources(p, n)):
                sp.dma_start(to[s][0:DH, :, at].bitcast(F32), of[1]).then_inc(one_in[s][n], 16)

        def load_gates(sp, p, s, n):
            at = slice(n * BLK, (n + 1) * BLK)
            sp.dma_start(K1[s][DH:DH + 2, :, at].bitcast(F32), s_Fp[bass.ds(p * 2, 2), :, at].rearrange("h w t -> w h t"))\
              .then_inc(one_in[s][n], 16)

        def load_two(sp, p, s, n):
            at = slice(n * BLK, (n + 1) * BLK)
            pair = bass.ds(p * (2 * P), 2 * P)
            queries = sources(p, n)[1]
            for to, of in ((K2[s][:, :, at].bitcast(F32), s_K[pair, at].rearrange("(h p) t -> p h t", p=P)),
                           (Q2[s][0:DH, :, at].bitcast(F32), queries[1]), (Q2[s][DH:P, :, at].bitcast(F32), queries[0]),
                           (V[s][:, n * NQ:(n + 1) * NQ], s_V[at, bass.ds(p * P, P)].rearrange("(k t) d -> t k d", t=P)),
                           (Z[s][:, at], s_ZT[bass.ds(p * P, P), at])):
                sp.dma_start(to, of).then_inc(two_in[s][n], 16)

        @block.sync
        def _(sp):
            for s in range(2):
                for n in range(NB):
                    load_one(sp, s, s, n)
                sp.wait_ge(rows_set[s], 2)
                for n in range(NB):
                    load_gates(sp, s, s, n)
                for n in range(NB):
                    load_two(sp, s, s, n)

            def store(p, s, load_next):
                for m, n in enumerate(reversed(range(NB))):
                    if load_next:
                        gated.wait(sp, p, m)
                        sp.sem_inc(sp_passed, 1)
                        for part in (load_one, load_gates, load_two):
                            part(sp, p + 2, s, n)
                    u_ok.wait(sp, p, m)
                    sp.sem_inc(sp_passed, 1)
                    sp.dma_start(s_u2T[bass.ds(p * P, P), n * BLK:(n + 1) * BLK], u[:, m % 2]).then_inc(u_stored[m % 2], 16)

            with sp.Fori(0, PAIRS // 2 - 1) as i:
                for s in range(2):
                    store(i * 2 + s, s, True)
            for p in range(PAIRS - 2, PAIRS):
                store(p, p % 2, False)
            for s in range(2):
                sp.wait_ge(u_stored[s], 16 * (PAIRS * NB // 2 + 1))

        def max_steps(j):
            span = MAX_END - MAX_START
            return range((j - MAX_START) * MAXS // span, (j + 1 - MAX_START) * MAXS // span) if MAX_START <= j < MAX_END else ()

        def rough_bank(j, alone):
            return (logits if alone and j % 4 >= 2 else rough)[:, j % 2]

        def rough_logits(pe, p, i, s, j, alone=False):
            qb, h, sub, grp = MAXI[j]
            if j == 0 or qb != MAXI[j - 1][0]:
                pe.wait_ge(one_in[s][qb], i * ONE + ONE)
            width = BLK if grp < qb else (sub + 1) * P
            q_at = slice(qb * BLK + sub * P, qb * BLK + (sub + 1) * P)
            reduced.wait(pe, p, max(j - 4, -2) if alone else j - 2)
            bank = rough_bank(j, alone)
            ins = nc.tensor.matmul(bank[:, 0:width], Q1[s][0:DH + 2, h, q_at],
                                   K1[s][0:DH + 2, h, grp * BLK:grp * BLK + width], start=True, stop=grp < qb)
            if grp == qb:
                ins = nc.tensor.matmul(bank[:, sub * P:width], ident_b[:, :], mask_q[:, :], start=False, stop=True)
            rough_ok.done(ins)

        def reduce(dve, p, j, alone=False):
            qb, h, sub, grp = MAXI[j]
            width = BLK if grp < qb else (sub + 1) * P
            if j == 0:
                top_ok.wait(dve, p, -1)
            rough_ok.wait(dve, p, j)
            reduced.done(nc.vector.tensor_reduce(partial[:, h, qb * NQ + sub, grp:grp + 1], rough_bank(j, alone)[:, 0:width],
                                                 AX.X, ALU.max))
            if j == MAXS - 1:
                reduced.wait(dve, p, j)
                minus_ok.wait(dve, p, -1)
                top_ok.done(nc.vector.tensor_reduce(top[:, :], partial[:, :, :, :].rearrange("p h t g -> p (h t) g"),
                                                    AX.X, ALU.max))

        def turn_top(pe, p):
            top_ok.wait(pe, p, 0)
            minus_ok.wait(pe, p, -1)
            top_turned_ok.done(nc.tensor.transpose(top_turned[0:2 * NT, 0:P], top[:, :], ident[:, :]))

        def negate_top(act, p):
            top_turned_ok.wait(act, p, 0)
            minus_ok.done(nc.scalar.activation(minus_top[:, :], top_turned[0:2 * NT, 0:P], ACT.Copy, scale=-1.0))

        def exact_logits(pe, p, j, h, s):
            qb, kb = MAIN[j]
            off = width_from(j)
            q_at, k_at = slice(qb * BLK + off, (qb + 1) * BLK), slice(kb * P, (kb + 1) * P)
            probs_ok.wait(pe, p, 2 * j + h - 2)
            out = logits[:, h, off:BLK]
            nc.tensor.matmul(out, K1[s][0:DH + 3, h, k_at], Q1[s][0:DH + 3, h, q_at], start=True, stop=False)
            if kb >= qb * NQ:
                nc.tensor.matmul(logits[:, h, off:off + P], ident_b[:, :], mask_k[:, :], start=False, stop=False)
            logits_ok.done(nc.tensor.matmul(out, K2[s][:, h, k_at], Q2[s][:, h, q_at], start=False, stop=True))

        def sum_values(pe, p, j, s):
            qb, kb = MAIN[j]
            m = NB - 1 - qb
            off = width_from(j)
            if kb == 0:
                gated.wait(pe, p, m - 2)
            probs_ok.wait(pe, p, 2 * j + 1)
            for h in range(2):
                at = slice(h * DH, (h + 1) * DH)
                ins = nc.tensor.matmul(o[at, m % 2, off:BLK], V[s][:, kb, at], probs[:, j % 3, h, off:BLK],
                                       start=kb == 0, stop=kb == NQ * (qb + 1) - 1)
            pv_ok.done(ins)

        def sum_tiles(pe, p, m):
            if m < NB - 1:
                joined.wait(pe, p, 2 * m + 1)
            else:
                v_summed.wait(pe, p, len(ON_DVE) - 1)
            if m:
                inv_ok.wait(pe, p, m - 1)
            for h in range(2):
                ins = nc.tensor.matmul(total[h * DH:(h + 1) * DH], ones[:, :], sum_v[:, m % 2, h], start=True, stop=True)
            total_ok.done(ins)

        @block.tensor
        def _(pe):
            pe.wait_ge(consts, 2)
            for j in range(MAXS):
                rough_logits(pe, 0, 0, 0, j, True)
            turn_top(pe, 0)

            def body(p, i, s, more):
                for n in range(NB):
                    pe.wait_ge(two_in[s][n], i * TWO + TWO)
                pe.wait_ge(top_in, p * 32 + 32)
                for j in range(STEPS + 3):
                    roughs = list(max_steps(j)) if more else []
                    for h in range(2):
                        if j < STEPS:
                            exact_logits(pe, p, j, h, s)
                        for r in roughs[h:h + 1]:
                            rough_logits(pe, p + 1, i + s, 1 - s, r)
                    if 1 <= j <= STEPS:
                        sum_values(pe, p, j - 1, s)
                    for r in roughs[2:]:
                        rough_logits(pe, p + 1, i + s, 1 - s, r)
                    for m in late(j, 3):
                        sum_tiles(pe, p, m)
                    if more and j == MAX_END + 1:
                        turn_top(pe, p + 1)

            over_pairs(pe, body)

        @block.vector
        def _(dve):
            v = nc.vector
            for x in (K1, Q1):
                v.memset(x[0][DH:DH + 3].bitcast(F32), 1.0).then_inc(rows_set[0], 1)
            dve.wait_ge(consts, 2)
            for j in range(MAXS):
                reduce(dve, 0, j, True)

            def add_up(p, j, h):
                qb, kb = MAIN[j]
                m, off, at = NB - 1 - qb, width_from(j), ON_DVE.index((j, h))
                probs_ok.wait(dve, p, 2 * j + h)
                x, to = probs[:, j % 3, h, off:BLK], sum_v[:, m % 2, h, off:BLK]
                if kb == 0:
                    total_ok.wait(dve, p, m - 2)
                    ins = v.tensor_copy(to, x)
                else:
                    v_summed.wait(dve, p, at - 2)
                    ins = v.tensor_tensor(to, to, x, ALU.add)
                v_summed.done(ins)

            def join(p, m):
                for h in range(2):
                    g_summed.wait(dve, p, max(n for n, (j, hh) in enumerate(ON_POOL) if hh == h and MAIN[j][0] == NB - 1 - m))
                    v_summed.wait(dve, p, max(n for n, (j, hh) in enumerate(ON_DVE) if hh == h and MAIN[j][0] == NB - 1 - m))
                    joined.done(v.tensor_tensor(sum_v[:, m % 2, h], sum_v[:, m % 2, h], sum_g[:, h], ALU.add))

            def gate(p, i, s, m):
                n = NB - 1 - m
                pv_ok.wait(dve, p, ENDS[m])
                dve.wait_ge(two_in[s][n], i * TWO + TWO)
                dve.wait_ge(u_stored[m % 2], p * (16 * NB // 2) + 16 * (m // 2 + 1))
                gated.done(v.tensor_tensor(u[:, m % 2], o[:, m % 2], Z[s][:, n * BLK:(n + 1) * BLK], ALU.mult))

            def normalize(p, m):
                inv_ok.wait(dve, p, m)
                gated.wait(dve, p, m)
                u_ok.done(v.tensor_tensor(u[:, m % 2], u[:, m % 2], inv[:, :], ALU.mult))

            def body(p, i, s, more):
                for j in range(STEPS + 5):
                    roughs = list(max_steps(j)) if more else []
                    for r in roughs[:2]:
                        reduce(dve, p + 1, r)
                    for h in range(2):
                        if (j, h) in ON_DVE:
                            add_up(p, j, h)
                    for r in roughs[2:]:
                        reduce(dve, p + 1, r)
                    for m in late(j, 1):
                        if m < NB - 1:
                            join(p, m)
                    for m in late(j, 2):
                        gate(p, i, s, m)
                    for m in late(j, 4):
                        normalize(p, m)

            over_pairs(dve, body)

        @block.scalar
        def _(act):
            act.preload_act_table_set("natural_log_exp_and_others")
            negate_top(act, 0)

            def summed(p, j, h):
                if (j % STEPS, h) in ON_POOL:
                    g_summed.wait(act, p, ON_POOL.index((j, h)))
                else:
                    v_summed.wait(act, p, ON_DVE.index((j % STEPS, h)) - (len(ON_DVE) if j < 0 else 0))

            def body(p, i, s, more):
                for j in range(STEPS + 4):
                    if j < STEPS:
                        off = width_from(j)
                        for h in range(2):
                            logits_ok.wait(act, p, 2 * j + h)
                            pv_ok.wait(act, p, j - 3)
                            summed(p, j - 3, h)
                            probs_ok.done(nc.scalar.activation(probs[:, j % 3, h, off:BLK], logits[:, h, off:BLK], ACT.Exp))
                    for m in late(j, 3):
                        total_ok.wait(act, p, m)
                        u_ok.wait(act, p, m - 1)
                        logged.done(nc.scalar.activation(inv[:, :], total[:, :], ACT.Ln))
                        logged.wait(act, p, m)
                        inv_ok.done(nc.scalar.activation(inv[:, :], inv[:, :], ACT.Exp, scale=-1.0))
                    if more and j == MAX_END + 1:
                        act.wait_ge(top_in, p * 32 + 32)
                        negate_top(act, p + 1)

            over_pairs(act, body)


_INS = ["x", "c", "a_mod_w", "a_mod_b", "a_pre_g", "a_post_g", "a_w_in", "a_conv_w", "a_a_log", "a_dt_bias",
        "a_o_gain", "a_w_out", "kv_mod_w", "kv_mod_b", "kv_norm_g", "kv_w", "kv_b_f",
        "b_mod_w", "b_mod_b", "b_pre_g", "b_post_g", "b_w_in", "b_w_out"]


def build(nc, a, out):
    dram = lambda name, shape, dt=F32: nc.dram_tensor(name, shape, dt).ap()
    s_mod = dram("s_mod", (1, 8 * D))
    s_xnT = dram("s_xnT0", (D, SEQ))
    s_qkv = dram("s_qkv", (3 * D + P, SEQ))
    s_zT = dram("s_zT", (D, SEQ))
    s_abT = dram("s_abT", (2 * AH, SEQ))
    begin(nc, a["c_cols"], [(a["a_mod_w"][0], a["a_mod_b"][0]), (a["kv_mod_w"], a["kv_mod_b"]),
                            (a["b_mod_w"][0], a["b_mod_b"][0])], s_mod, a["x"], s_xnT)
    deltanet_projection(nc, s_xnT, s_mod, a["a_pre_cols"], a["a_w_in"][0], a["taps"], s_qkv, s_zT, s_abT)
    s_g, s_uT = dram("s_g", (AH, SEQ)), dram("s_uT", (D, SEQ))
    delta_rule(nc, s_qkv, s_zT, s_abT, a["a_log_col"], a["dt_bias_col"], a["o_gain_col"], a["level_masks"], s_g, s_uT)
    s_x1, s_xnT1 = dram("s_x1", (SEQ, D)), dram("s_xnT", (D, SEQ))
    output_projection(nc, "oa", s_uT, a["a_w_out"][0], s_mod, 2 * D, a["a_post_g"], a["x"][0], s_x1, s_xnT1)
    s_K, s_V = dram("s_K", (BH * P, SEQ)), dram("s_V", (SEQ, D))
    s_F_raw, s_F = dram("s_F_raw", (BH, SEQ)), dram("s_Fp", (BH, 2, SEQ))
    plain_projection(nc, "pk", s_xnT1, s_mod, a["kv_norm_cols"], 3 * D, 4 * D, a["kv_w"], 1.0, s_K, "by token", s_V,
                     gates=(a["kv_b_f_col"], s_F_raw))
    s_Q, s_ZT = dram("s_Q", (BH * P, SEQ)), dram("s_ZT", (D, SEQ))
    plain_projection(nc, "pb", s_xnT1, s_mod, a["b_pre_cols"], 5 * D, 6 * D, a["b_w_in"][0], DH ** -0.5, s_Q, "silu", s_ZT,
                     finish=(s_F_raw, s_F))
    s_u2T = dram("s_u2T", (D, SEQ))
    nc.disable_value_cache = True
    attention(nc, s_K, s_F, s_V, s_Q, s_ZT, s_u2T)
    nc.disable_value_cache = False
    output_projection(nc, "ob", s_u2T, a["b_w_out"][0], s_mod, 7 * D, a["b_post_g"], s_x1, out[0], None)


def kernel(**inputs):
    import numpy as np
    import concourse.bacc as bacc
    from concourse.bass_utils import run_bass_kernel_spmd

    nc = bacc.Bacc("TRN2", target_bir_lowering=False, num_devices=1)
    arrays, aps = {}, {}

    def give(name, array):
        array = np.ascontiguousarray(array)
        arrays[f"in_{name}_dram"] = array
        aps[name] = nc.dram_tensor(f"in_{name}_dram", array.shape, mybir.dt.from_np(array.dtype), kind="ExternalInput").ap()

    for name in _INS:
        give(name, inputs[name])
    give("taps", np.asarray(inputs["a_conv_w"])[0].reshape(4, 3 * AH, P).transpose(2, 1, 0))
    for name, of in (("c_cols", "c"), ("a_pre_cols", "a_pre_g"), ("kv_norm_cols", "kv_norm_g"), ("b_pre_cols", "b_pre_g")):
        give(name, np.asarray(inputs[of]).reshape(KC, P).T)
    for name, of in (("a_log_col", "a_a_log"), ("dt_bias_col", "a_dt_bias"), ("o_gain_col", "a_o_gain"), ("kv_b_f_col", "kv_b_f")):
        give(name, np.asarray(inputs[of]).reshape(-1, 1))
    row, col = np.arange(P)[:, None], np.arange(P)[None, :]
    above = [((col >> l) == (row >> l) + 1) & ((col >> l) % 2 == 1) for l in range(7)]
    give("level_masks", np.stack(above, axis=1).astype(np.float32))
    out = nc.dram_tensor("out_0_dram", (1, SEQ, D), F32, kind="ExternalOutput").ap()
    build(nc, aps, out)
    result = run_bass_kernel_spmd(nc, [arrays], core_ids=[0])
    return result.results[0]["out_0_dram"]
```
